# Optimizing a Trainium2 kernel written in Bass

```python
import math
import jax, jax.numpy as jnp
from jax import lax
import numpy as np

D_MODEL = 1024
BATCH = 1
SEQ = 512
DEPTH = 2

MIX_WIDTH = D_MODEL
HEAD_DIM = 64
N_HEADS_DIFF = MIX_WIDTH // (4 * HEAD_DIM)
N_HEADS_FOX = MIX_WIDTH // (2 * HEAD_DIM)
DIFF_WIDTH = N_HEADS_DIFF * 2 * HEAD_DIM
FOX_WIDTH = N_HEADS_FOX * HEAD_DIM
IN_WIDTH = 3 * DIFF_WIDTH + 3 * FOX_WIDTH + N_HEADS_FOX
ROT_DIM = HEAD_DIM // 4
ROPE_THETA = 500000.0
Q_BLOCK = 128
D_FF = ((8 * D_MODEL // 3 + 255) // 256) * 256
EPS = 1e-6
NEG_INF = -1e30


def rms_norm(x, g):
    xf = x.astype(jnp.float32)
    y = xf * lax.rsqrt(jnp.mean(xf * xf, axis=-1, keepdims=True) + EPS)
    return (y * g.astype(jnp.float32)).astype(x.dtype)

def rotary_tables(positions, dtype):
    inv_freq = 1.0 / (ROPE_THETA ** (jnp.arange(0, ROT_DIM, 2, dtype=jnp.float32) / ROT_DIM))
    ang = positions.astype(jnp.float32)[..., None] * inv_freq
    cos = jnp.cos(ang)[:, :, None, :].astype(dtype)
    sin = jnp.sin(ang)[:, :, None, :].astype(dtype)
    return cos, sin

def partial_rotary(t, cos, sin):
    half = ROT_DIM // 2
    t1, t2, rest = t[..., :half], t[..., half:ROT_DIM], t[..., ROT_DIM:]
    return jnp.concatenate([t1 * cos - t2 * sin, t2 * cos + t1 * sin, rest], axis=-1)

def diff_attention(q, k, v, lam):
    b, s = q.shape[0], q.shape[1]
    nb = s // Q_BLOCK
    scale = HEAD_DIM ** -0.5
    q_blocks = q.reshape(b, nb, Q_BLOCK, N_HEADS_DIFF, 2, HEAD_DIM).swapaxes(0, 1)
    k_pos = jnp.arange(s)

    def block(args):
        i, qi = args
        q_pos = i * Q_BLOCK + jnp.arange(Q_BLOCK)
        causal = q_pos[:, None] >= k_pos[None, :]
        logits = jnp.einsum('bqhmd,bkhmd->bhmqk', qi, k).astype(jnp.float32) * scale
        logits = jnp.where(causal, logits, NEG_INF)
        p = jax.nn.softmax(logits, axis=-1)
        p = p[:, :, 0] - lam * p[:, :, 1]
        return jnp.einsum('bhqk,bkhe->bqhe', p.astype(v.dtype), v)

    o = lax.map(block, (jnp.arange(nb), q_blocks))
    return o.swapaxes(0, 1).reshape(b, s, N_HEADS_DIFF, 2 * HEAD_DIM)

def forgetting_attention(q, k, v, log_f):
    b, s = q.shape[0], q.shape[1]
    nb = s // Q_BLOCK
    scale = HEAD_DIM ** -0.5
    c = jnp.cumsum(log_f, axis=1)
    c_k = c.transpose(0, 2, 1)[:, :, None, :]
    q_blocks = q.reshape(b, nb, Q_BLOCK, N_HEADS_FOX, HEAD_DIM).swapaxes(0, 1)
    c_blocks = c.reshape(b, nb, Q_BLOCK, N_HEADS_FOX).swapaxes(0, 1)
    k_pos = jnp.arange(s)

    def block(args):
        i, qi, ci = args
        q_pos = i * Q_BLOCK + jnp.arange(Q_BLOCK)
        causal = q_pos[:, None] >= k_pos[None, :]
        decay = ci.transpose(0, 2, 1)[..., None] - c_k
        logits = jnp.einsum('bqhd,bkhd->bhqk', qi, k).astype(jnp.float32) * scale + decay
        logits = jnp.where(causal, logits, NEG_INF)
        p = jax.nn.softmax(logits, axis=-1)
        return jnp.einsum('bhqk,bkhd->bqhd', p.astype(v.dtype), v)

    o = lax.map(block, (jnp.arange(nb), q_blocks, c_blocks))
    return o.swapaxes(0, 1).reshape(b, s, N_HEADS_FOX, HEAD_DIM)

def first_inputs(seed: int = 0) -> dict:
    key = jax.random.key(seed)
    ks = jax.random.split(key, 16)
    f32 = jnp.float32

    def nrm(k, shape, scale):
        return jax.random.normal(k, shape, f32) * scale

    def gain(k, n):
        return 1.0 + 0.05 * jax.random.normal(k, (DEPTH, n), f32)

    return {
        "x": nrm(ks[0], (BATCH, SEQ, D_MODEL), 1.0),
        "positions": jnp.broadcast_to(jnp.arange(SEQ, dtype=jnp.int32), (BATCH, SEQ)),
        "attn_pre_g": gain(ks[1], D_MODEL),
        "w_in": nrm(ks[2], (DEPTH, D_MODEL, IN_WIDTH), D_MODEL ** -0.5),
        "forget_bias": jax.random.uniform(ks[3], (DEPTH, N_HEADS_FOX), f32, 1.0, 6.0),
        "lam_q1": nrm(ks[4], (DEPTH, HEAD_DIM), 0.1),
        "lam_k1": nrm(ks[5], (DEPTH, HEAD_DIM), 0.1),
        "lam_q2": nrm(ks[6], (DEPTH, HEAD_DIM), 0.1),
        "lam_k2": nrm(ks[7], (DEPTH, HEAD_DIM), 0.1),
        "diff_sub_g": gain(ks[8], 2 * HEAD_DIM),
        "w_out": nrm(ks[9], (DEPTH, MIX_WIDTH, D_MODEL), MIX_WIDTH ** -0.5),
        "attn_post_g": gain(ks[10], D_MODEL),
        "ffn_pre_g": gain(ks[11], D_MODEL),
        "w_gate": nrm(ks[12], (DEPTH, D_MODEL, D_FF), D_MODEL ** -0.5),
        "w_up": nrm(ks[13], (DEPTH, D_MODEL, D_FF), D_MODEL ** -0.5),
        "w_down": nrm(ks[14], (DEPTH, D_FF, D_MODEL), D_FF ** -0.5),
        "ffn_post_g": gain(ks[15], D_MODEL),
    }

def first_block(x, positions, attn_pre_g, w_in, forget_bias, lam_q1, lam_k1, lam_q2, lam_k2,
              diff_sub_g, w_out, attn_post_g, ffn_pre_g, w_gate, w_up, w_down, ffn_post_g):
    b, s, _ = x.shape
    f32 = jnp.float32
    cos, sin = rotary_tables(positions, x.dtype)
    split_at = [DIFF_WIDTH, 2 * DIFF_WIDTH, 3 * DIFF_WIDTH,
                3 * DIFF_WIDTH + FOX_WIDTH, 3 * DIFF_WIDTH + 2 * FOX_WIDTH,
                3 * DIFF_WIDTH + 3 * FOX_WIDTH]
    for l in range(DEPTH):
        h = rms_norm(x, attn_pre_g[l])
        proj = h @ w_in[l]
        qa, ka, va, qb, kb, vb, f_logit = jnp.split(proj, split_at, axis=-1)

        qa = partial_rotary(qa.reshape(b, s, 2 * N_HEADS_DIFF, HEAD_DIM), cos, sin)
        ka = partial_rotary(ka.reshape(b, s, 2 * N_HEADS_DIFF, HEAD_DIM), cos, sin)
        qa = qa.reshape(b, s, N_HEADS_DIFF, 2, HEAD_DIM)
        ka = ka.reshape(b, s, N_HEADS_DIFF, 2, HEAD_DIM)
        va = va.reshape(b, s, N_HEADS_DIFF, 2 * HEAD_DIM)
        lam_init = 0.8 - 0.6 * math.exp(-0.3 * l)
        lam = (jnp.exp(jnp.sum(lam_q1[l].astype(f32) * lam_k1[l].astype(f32)))
               - jnp.exp(jnp.sum(lam_q2[l].astype(f32) * lam_k2[l].astype(f32)))
               + lam_init)
        oa = diff_attention(qa, ka, va, lam)
        oa = rms_norm(oa, diff_sub_g[l]) * (1.0 - lam_init)

        log_f = jax.nn.log_sigmoid(f_logit.astype(f32) + forget_bias[l].astype(f32))
        ob = forgetting_attention(qb.reshape(b, s, N_HEADS_FOX, HEAD_DIM),
                                  kb.reshape(b, s, N_HEADS_FOX, HEAD_DIM),
                                  vb.reshape(b, s, N_HEADS_FOX, HEAD_DIM), log_f)

        mixed = jnp.concatenate([oa.reshape(b, s, DIFF_WIDTH), ob.reshape(b, s, FOX_WIDTH)], axis=-1)
        x = x + rms_norm(mixed @ w_out[l], attn_post_g[l])

        h = rms_norm(x, ffn_pre_g[l])
        y = (jax.nn.silu(h @ w_gate[l]) * (h @ w_up[l])) @ w_down[l]
        x = x + rms_norm(y, ffn_post_g[l])
    return x


DEPTH_2 = 1

SB_HEADS = 8
SB_HEAD_DIM = 64
SB_WIDTH = SB_HEADS * SB_HEAD_DIM
HG_HEADS = 4
HG_KEY_DIM = 128
HG_VAL_DIM = 128
HG_KEY_WIDTH = HG_HEADS * HG_KEY_DIM
HG_WIDTH = HG_HEADS * HG_VAL_DIM
HG_CHUNK = 64
MIX_WIDTH_2 = SB_WIDTH + HG_WIDTH
FFN_HIDDEN = -(-8 * D_MODEL // (3 * 256)) * 256
IN_SIZES = (SB_WIDTH, SB_WIDTH, SB_WIDTH, HG_KEY_WIDTH, HG_KEY_WIDTH,
            HG_WIDTH, HG_WIDTH, D_MODEL, D_MODEL)
IN_WIDTH_2 = sum(IN_SIZES)


def rms_norm_2(x, g):
    xf = x.astype(jnp.float32)
    y = xf * lax.rsqrt(jnp.mean(xf * xf, axis=-1, keepdims=True) + EPS)
    return (y * g.astype(jnp.float32)).astype(x.dtype)

def split_cols(t, sizes):
    idx, acc = [], 0
    for s in sizes[:-1]:
        acc += s
        idx.append(acc)
    return jnp.split(t, idx, axis=-1)

def stick_breaking_attention(q, k, v):
    seq = q.shape[2]
    scale = SB_HEAD_DIM ** -0.5
    outs = []
    for blk in range(seq // Q_BLOCK):
        t0 = blk * Q_BLOCK
        end = t0 + Q_BLOCK
        qb, kb, vb = q[:, :, t0:end], k[:, :, :end], v[:, :, :end]
        z = jnp.einsum('bhtd,bhsd->bhts', qb, kb).astype(jnp.float32) * scale
        t_idx = t0 + jnp.arange(Q_BLOCK)[:, None]
        s_idx = jnp.arange(end)[None, :]
        causal = s_idx < t_idx
        sp = jnp.where(causal, jax.nn.softplus(z), 0.0)
        rest = lax.cumsum(sp, axis=3, reverse=True) - sp
        w = jnp.where(causal, jnp.exp(jax.nn.log_sigmoid(z) - rest), 0.0)
        outs.append(jnp.einsum('bhts,bhsd->bhtd', w.astype(vb.dtype), vb))
    return jnp.concatenate(outs, axis=2)

def hgrn2_mixer(q_in, f_in, i_in, g_in, lb, norm_g):
    B, S, _ = q_in.shape
    n_chunks = S // HG_CHUNK
    f = lb + (1.0 - lb) * jax.nn.sigmoid(f_in.astype(jnp.float32))
    log_f = jnp.log(f)
    key = 1.0 - f
    q = jax.nn.silu(q_in.astype(jnp.float32))
    val = i_in.astype(jnp.float32)

    def to_chunks(t):
        return t.reshape(B, n_chunks, HG_CHUNK, HG_HEADS, -1).transpose(1, 0, 3, 2, 4)

    mask = jnp.tril(jnp.ones((HG_CHUNK, HG_CHUNK), dtype=bool))[:, :, None]

    def step(state, xs):
        qc, kc, vc, gc = xs
        b = jnp.cumsum(gc, axis=2)
        diff = b[:, :, :, None, :] - b[:, :, None, :, :]
        decay = jnp.exp(jnp.where(mask, diff, -jnp.inf))
        attn = jnp.einsum('bhtk,bhsk,bhtsk->bhts', qc, kc, decay)
        o_intra = jnp.einsum('bhts,bhsv->bhtv', attn, vc)
        o_inter = jnp.einsum('bhtk,bhkv->bhtv', qc * jnp.exp(b), state)
        b_last = b[:, :, -1:, :]
        new_state = jnp.exp(b_last[:, :, 0, :])[..., None] * state + \
            jnp.einsum('bhsk,bhsv->bhkv', kc * jnp.exp(b_last - b), vc)
        return new_state, o_intra + o_inter

    s0 = jnp.zeros((B, HG_HEADS, HG_KEY_DIM, HG_VAL_DIM), jnp.float32)
    _, o = lax.scan(step, s0, (to_chunks(q), to_chunks(key), to_chunks(val), to_chunks(log_f)))
    o = o.transpose(1, 0, 3, 2, 4).reshape(B, S, HG_HEADS, HG_VAL_DIM)
    o = rms_norm_2(o, norm_g)
    gate = jax.nn.silu(g_in.astype(jnp.float32)).reshape(B, S, HG_HEADS, HG_VAL_DIM)
    return (o * gate).reshape(B, S, HG_WIDTH).astype(q_in.dtype)

def hybrid_layer(x, norm1_g, w_in, q_norm_g, k_norm_g, lb, hg_norm_g, w_branch, w_out,
                 norm2_g, w_gate, w_up, w_down):
    B, S, _ = x.shape
    xn = rms_norm_2(x, norm1_g)
    proj = xn @ w_in
    q_sb, k_sb, v_sb, q_hg, f_hg, i_hg, g_hg, gate_sb, gate_hg = split_cols(proj, IN_SIZES)

    def heads(t):
        return t.reshape(B, S, SB_HEADS, SB_HEAD_DIM).transpose(0, 2, 1, 3)

    q = rms_norm_2(heads(q_sb), q_norm_g)
    k = rms_norm_2(heads(k_sb), k_norm_g)
    o_sb = stick_breaking_attention(q, k, heads(v_sb))
    o_sb = o_sb.transpose(0, 2, 1, 3).reshape(B, S, SB_WIDTH)

    o_hg = hgrn2_mixer(q_hg, f_hg, i_hg, g_hg, lb, hg_norm_g)

    y_sb = o_sb @ w_branch[:SB_WIDTH]
    y_hg = o_hg @ w_branch[SB_WIDTH:]
    mixed = jax.nn.sigmoid(gate_sb) * y_sb + jax.nn.sigmoid(gate_hg) * y_hg
    h = x + mixed @ w_out

    hn = rms_norm_2(h, norm2_g)
    ffn = (jax.nn.silu(hn @ w_gate) * (hn @ w_up)) @ w_down
    return h + ffn

def second_inputs(seed: int = 0) -> dict:
    key = jax.random.key(seed)
    ks = jax.random.split(key, 13)
    n = jax.random.normal
    f32 = jnp.float32
    return {
        "x": n(ks[0], (BATCH, SEQ, D_MODEL), f32),
        "norm1_g": 1.0 + 0.02 * n(ks[1], (DEPTH_2, D_MODEL), f32),
        "w_in": n(ks[2], (DEPTH_2, D_MODEL, IN_WIDTH_2), f32) * D_MODEL ** -0.5,
        "q_norm_g": 1.0 + 0.02 * n(ks[3], (DEPTH_2, SB_HEAD_DIM), f32),
        "k_norm_g": 1.0 + 0.02 * n(ks[4], (DEPTH_2, SB_HEAD_DIM), f32),
        "lb_table": 0.5 * n(ks[5], (DEPTH_2 + 1, HG_KEY_WIDTH), f32),
        "hg_norm_g": 1.0 + 0.02 * n(ks[6], (DEPTH_2, HG_VAL_DIM), f32),
        "w_branch": n(ks[7], (DEPTH_2, MIX_WIDTH_2, D_MODEL), f32) * SB_WIDTH ** -0.5,
        "w_out": n(ks[8], (DEPTH_2, D_MODEL, D_MODEL), f32) * D_MODEL ** -0.5,
        "norm2_g": 1.0 + 0.02 * n(ks[9], (DEPTH_2, D_MODEL), f32),
        "w_ffn_gate": n(ks[10], (DEPTH_2, D_MODEL, FFN_HIDDEN), f32) * D_MODEL ** -0.5,
        "w_ffn_up": n(ks[11], (DEPTH_2, D_MODEL, FFN_HIDDEN), f32) * D_MODEL ** -0.5,
        "w_ffn_down": n(ks[12], (DEPTH_2, FFN_HIDDEN, D_MODEL), f32) * FFN_HIDDEN ** -0.5,
    }

def second_block(x, norm1_g, w_in, q_norm_g, k_norm_g, lb_table, hg_norm_g, w_branch, w_out,
              norm2_g, w_ffn_gate, w_ffn_up, w_ffn_down):
    lower_bounds = jnp.cumsum(jax.nn.softmax(lb_table.astype(jnp.float32), axis=0), axis=0)
    h = x
    for layer in range(DEPTH_2):
        h = hybrid_layer(h, norm1_g[layer], w_in[layer], q_norm_g[layer], k_norm_g[layer],
                         lower_bounds[layer], hg_norm_g[layer], w_branch[layer], w_out[layer],
                         norm2_g[layer], w_ffn_gate[layer], w_ffn_up[layer], w_ffn_down[layer])
    return h


def setup_inputs(seed=0):
    out = dict(first_inputs(seed))
    for name, value in second_inputs(seed + 1).items():
        if name != "x":
            out[name + "_2"] = value
    return out


def reference(
    x, positions, attn_pre_g, w_in, forget_bias, lam_q1, lam_k1, lam_q2, lam_k2, diff_sub_g,
    w_out, attn_post_g, ffn_pre_g, w_gate, w_up, w_down, ffn_post_g, norm1_g_2, w_in_2,
    q_norm_g_2, k_norm_g_2, lb_table_2, hg_norm_g_2, w_branch_2, w_out_2, norm2_g_2,
    w_ffn_gate_2, w_ffn_up_2, w_ffn_down_2,
):
    x = first_block(
        x, positions, attn_pre_g, w_in, forget_bias, lam_q1, lam_k1, lam_q2, lam_k2, diff_sub_g,
        w_out, attn_post_g, ffn_pre_g, w_gate, w_up, w_down, ffn_post_g,
    )
    return second_block(
        x, norm1_g_2, w_in_2, q_norm_g_2, k_norm_g_2, lb_table_2, hg_norm_g_2, w_branch_2,
        w_out_2, norm2_g_2, w_ffn_gate_2, w_ffn_up_2, w_ffn_down_2,
    )


_drawn_inputs = setup_inputs


def setup_inputs(seed=0):
    import zlib

    import numpy as np

    out = dict(_drawn_inputs(seed))
    spreads = {}
    factors = {'norm1_g_2': 8.0,
     'q_norm_g_2': 26.425,
     'k_norm_g_2': 27.515,
     'lb_table_2': 8.0,
     'hg_norm_g_2': 8.0,
     'norm2_g_2': 7.617}
    for name, (base, spread) in spreads.items():
        noise = np.random.default_rng([zlib.crc32(name.encode()), seed]).standard_normal(out[name].shape)
        drawn = base * np.exp(spread * noise) if base else spread * noise
        out[name] = __import__('jax').numpy.asarray(drawn.astype(out[name].dtype))
    for name, factor in factors.items():
        out[name] = (out[name] * factor).astype(out[name].dtype)
    return out
```

```python
import math
from contextlib import ExitStack

import numpy as np
import concourse.bass as bass
from concourse import mybir

F32 = mybir.dt.float32
F32R = mybir.dt.float32r
BF16 = mybir.dt.bfloat16
I32 = mybir.dt.int32
ALU = mybir.AluOpType
ACT = mybir.ActivationFunctionType
AX = mybir.AxisListType

P = 128
SEQ = 512
D = 1024
DEPTH = 2
T = SEQ // P
KD = D // P
CW = 512
F = 2816
KF = F // P
HD = 64
NEG = -1.0e30
EPS = 1e-6
ROT = 8
THETA = 500000.0
LAM_INIT = [0.8 - 0.6 * math.exp(-0.3 * l) for l in range(DEPTH)]
R = 4
LEVELS = 7
EXP_TABLE = "natural_log_exp_and_others"

TWO_PI = []
_rest = 2 * math.pi
for _bits in (6, 6, 6):
    _e = math.floor(math.log2(_rest)) - _bits + 1
    _part = math.floor(_rest / 2.0 ** _e) * 2.0 ** _e
    TWO_PI.append(_part)
    _rest -= _part
TWO_PI.append(_rest)
PI_F32 = float(np.nextafter(np.float32(math.pi), np.float32(0)))
ROUND = 1.5 * 2 ** 23


def shape_constants():
    s = np.arange(P)[:, None]
    t = np.arange(P)[None, :]
    sums = [s <= t]
    pairs = [s == t]
    for level in range(LEVELS):
        h = 1 << level
        same = (s >> level) == (t >> level)
        right = ((t >> level) & 1) == 1
        sums.append(same & np.where(right, s <= t, s > t))
        pairs.append(right & (((s >> level) & 1) == 0) & ((s >> (level + 1)) == (t >> (level + 1))))
    sums += [s > t, s < t, s >= 0 * t]
    return {
        "identity": np.eye(P, dtype=np.float32),
        "causal": np.where(t > s, np.float32(NEG), np.float32(0)),
        "sums": np.stack(sums, 1).astype(np.float32),
        "pairs": np.stack(pairs, 1).astype(np.float32),
        "inv_freq": (1.0 / (np.float32(THETA) ** (np.arange(0, 2 * ROT, 2, dtype=np.float32) / np.float32(2 * ROT)))).astype(np.float32),
    }


UPTO = 0
AFTER = LEVELS + 1
BEFORE = LEVELS + 2
ONES = LEVELS + 3

STAGES = []
for _l in range(DEPTH):
    STAGES += [(f"in{_l}", 6), (f"out{_l}", 2), (f"ffn{_l}", 11), (f"down{_l}", 6)]
STAGES += [("in2", 11), ("branch2", 2), ("out2", 2), ("ffn2", 11), ("down2", 6)]
LAP0 = {}
_at = 0
for _name, _n in STAGES:
    LAP0[_name] = _at
    _at += _n
LAPS = dict(STAGES)
FFN_SEEN = {"ffn0": 0, "ffn1": 11, "ffn2": 22}
SETS = {"in": (3, 3), "out": (1, 1), "ffn": (0, 0), "down": (1, 1), "in2": (6, 5), "branch": (2, 2), "out2": (1, 0)}
SET0 = {}
_a, _b = 0, 0
for _name, _n in STAGES:
    SET0[_name] = (_a, _b)
    _k = SETS.get(_name) or SETS[_name[:-1]]
    _a, _b = _a + _k[0], _b + _k[1]
DOWN_SUBS = [2] * 10 + [1, 1]
assert sum(DOWN_SUBS) == KF


def build(nc, x, positions, attn_pre_g, w_in, forget_bias, lam_q1, lam_k1, lam_q2, lam_k2, diff_sub_g,
          w_out, attn_post_g, ffn_pre_g, w_gate, w_up, w_down, ffn_post_g, norm1_g_2, w_in_2,
          q_norm_g_2, k_norm_g_2, lb_table_2, hg_norm_g_2, w_branch_2, w_out_2, norm2_g_2,
          w_ffn_gate_2, w_ffn_up_2, w_ffn_down_2, identity, causal, sums, pairs, inv_freq, out):
    ctx = ExitStack()
    with ctx:
        def sb(name, shape, dt=F32, scope=ctx):
            return scope.enter_context(nc.sbuf_tensor(name, shape, dt))

        def sem(name):
            return ctx.enter_context(nc.semaphore(name))

        X = sb("X", [P, T, D])
        raw = sb("raw", [P, R, 2, CW])
        w_hi = sb("w_hi", [P, R, 2, CW], F32R)
        w_lo = sb("w_lo", [P, R, 2, CW], F32R)
        SUMS = sb("SUMS", [P, LEVELS + 4, P])
        PAIRS = sb("PAIRS", [P, LEVELS + 1, P], BF16)
        ident = sb("ident", [P, P])
        ident_b = sb("ident_b", [P, P], BF16)
        causal_b = sb("causal_b", [P, P], BF16)
        G = sb("G", [P, D])
        gcol = sb("gcol", [P, 10, KD])
        qkg = sb("qkg", [P, 2])
        cs = sb("cs", [P, 2, T, ROT])
        fw_hi = sb("fw_hi", [P, DEPTH, KD, 8], F32R)
        fw_lo = sb("fw_lo", [P, DEPTH, KD, 8], F32R)
        fbias = sb("fbias", [P, DEPTH, 8])
        lam = sb("lam", [P, DEPTH])
        small = sb("small", [P, 6, 32])
        ssq = sb("ssq", [P, 2, T])
        nmax = sb("nmax", [P, 4])
        rsum = sb("rsum", [P, 4])
        mark = sb("mark", [P, 4])
        fy = sb("fy", [P, 3, T, 8])

        r1 = ExitStack()
        xt_hi = sb("xt_hi", [P, KD, SEQ], F32R, r1)
        xt_lo = sb("xt_lo", [P, KD, SEQ], F32R, r1)
        r1.close()
        R1 = sb("R1", [P, 2 * KD * SEQ])
        r2 = ExitStack()
        ht_hi = sb("ht_hi", [P, KF, SEQ], F32R, r2)
        ht_lo = sb("ht_lo", [P, KF, SEQ], F32R, r2)
        silu_g = sb("silu_g", [P, 2, SEQ], F32, r2)
        h_tmp = sb("h_tmp", [P, SEQ], F32, r2)
        r2.close()
        R2 = sb("R2", [P, 24576])

        def at1(a, *dims):
            return view(R1, a, dims)

        def at2(a, *dims):
            return view(R2, a, dims)

        def view(tensor, a, dims):
            n = int(np.prod(dims))
            ap = tensor[:, a:a + n]
            if len(dims) == 2:
                return ap.rearrange("p (a b) -> p a b", b=dims[1])
            if len(dims) == 3:
                return ap.rearrange("p (a b c) -> p a b c", b=dims[1], c=dims[2])
            return ap

        XN = at2(0, T, D)
        QA = at2(0, T, CW)
        KA = at2(2048, T, CW)
        MIX = XN
        VA = at2(4096, T, 4, 129)
        QB = at2(6160, T, 8, 66)
        KB = at2(8272, T, 8, 66)
        VB = at2(10384, T, 8, 65)
        QAT = at2(12464, 4, SEQ)
        KAT = at2(14512, 4, SEQ)
        prob = at2(16560, 2, SEQ)
        probT = at2(17584, 2, SEQ)
        otmp = at2(18608, 2, P)
        SQ = at2(18864, T, CW)
        rot = at2(16560, 4, T, ROT * 8)
        QBT = at1(0, 8, SEQ)
        KBT = at1(4096, 8, SEQ)
        YG_out = at2(4096, T, D)
        YG_down = at1(0, T, D)
        junk_down = at1(4096, T, CW)
        SQ2 = at2(20480, T, CW)
        QS, KS, VS = at2(0, T, CW), at2(2048, T, CW), at2(4096, T, CW)
        QH, KEY, LOGF, VAL, GG = (at2(6144 + 2048 * n, T, CW) for n in range(5))
        GATE_SB, GATE_HG = at2(16384, T, D), at2(20480, T, D)
        QST, KST, QHT, KHT = (at1(2048 * n, 4, SEQ) for n in range(4))
        sb_l = at2(6144, 3, SEQ)
        sb_sp = at2(7680, 2, 1280)
        NE = LEVELS + 2
        hg_e = (at1(0, NE, P), at1(NE * P, NE, P))
        hg_q = (at2(6144, LEVELS + 1, P), at2(7168, LEVELS + 1, P))
        hg_k = (at2(8192, LEVELS + 1, P), at2(9216, LEVELS + 1, P))
        hg_a = at2(4096, LEVELS + 1, P)
        hg_at = at2(5120, 2, P)
        hg_ket = at2(5376, 2, P)
        hg_state = at1(2 * NE * P, 4, P)
        SQ3 = at1(0, T, CW)
        lb_tmp = at2(20480, 4, CW)
        pos_i = at2(12000, T).bitcast(I32)
        ang = at2(12016, 8, T, ROT)
        freq = at2(12304, ROT)
        fw_raw = at2(12320, DEPTH, KD, 8)
        causal_f = at2(12448, P)
        pairs_f = at2(12576, LEVELS + 1, P)
        lam_in = at2(13600, DEPTH * 4, HD)
        lam_s = at2(14112, 8)
        lam_t = at2(14120, DEPTH * 2, HD)

        PS = ctx.enter_context(nc.psum_tensor("PS", [P, 8, 512], F32))

        x_in = sem("x_in")
        const_in = sem("const_in")
        gain_in = sem("gain_in")
        raw_in = [sem(f"raw_in{r}") for r in range(R)]
        up_in = [sem(f"up_in{r}") for r in range(R)]
        hi_ready, lo_ready, w_used = sem("hi_ready"), sem("lo_ready"), sem("w_used")
        evac = [sem("evac0"), sem("evac1")]
        xn_ready, ts_mm, ts_hi, ts_lo = sem("xn_ready"), sem("ts_mm"), sem("ts_hi"), sem("ts_lo")
        x_ready, sq_done, ss_ready, y0_ready = sem("x_ready"), sem("sq_done"), sem("ss_ready"), sem("y0_ready")
        yg_done = sem("yg_done")
        silu_done, h_mul, h_hi, h_lo = sem("silu_done"), sem("h_mul"), sem("h_hi"), sem("h_lo")
        trig_done, lam_dots, lam_exps = sem("trig_done"), sem("lam_dots"), sem("lam_exps")
        small_consts, fw_done, first_in, lb_in = sem("small_consts"), sem("fw_done"), sem("first_in"), sem("lb_in")
        dve_step, act_step, pool_step = sem("dve_step"), sem("act_step"), sem("pool_step")
        qkv_done, qk2_done = sem("qkv_done"), sem("qk2_done")
        f_mm, f_biased, f_log, f_gate, c_mm, c_placed = (sem(n) for n in ("f_mm", "f_biased", "f_log", "f_gate", "c_mm", "c_placed"))
        tr_mm, tr_act, tr_dve = sem("tr_mm"), sem("tr_act"), sem("tr_dve")
        s_mm, max_done, exp_done, pt_mm, pt_ev, o_mm, o_norm = (
            sem(n) for n in ("s_mm", "max_done", "exp_done", "pt_mm", "pt_ev", "o_mm", "o_norm"))
        sq_ready = sem("sq_ready")
        out_done = sem("out_done")
        lb_max, lb_exp, lb_done = sem("lb_max"), sem("lb_exp"), sem("lb_done")
        sig_done, qk_copied, qk_sq, log_done, f_sum = (sem(n) for n in ("sig_done", "qk_copied", "qk_sq", "log_done", "f_sum"))
        z_mm, l_done, sp_done, rest_mm, arg_done, w_exp, w_mask, av_mm, av_ev = (
            sem(n) for n in ("z_mm", "l_done", "sp_done", "rest_mm", "arg_done", "w_exp", "w_mask", "av_mm", "av_ev"))
        e_mm, e_exp, qe_done, ke_done, a_mm, a_sum, ket_mm, ket_ev, kv_mm, state_done, oh_mm, oh_ev = (
            sem(n) for n in ("e_mm", "e_exp", "qe_done", "ke_done", "a_mm", "a_sum", "ket_mm", "ket_ev", "kv_mm",
                             "state_done", "oh_mm", "oh_ev"))
        a_read = sem("a_read")
        y_sb_done, final_ready = sem("y_sb_done"), sem("final_ready")

        const_total = []
        TS_OF = {"in0": 0, "out0": 1, "ffn0": 2, "in1": 3, "out1": 4, "ffn1": 5, "in2": 6, "branch2": 7, "out2": 8, "ffn2": 9}
        weights = {}
        for l in range(DEPTH):
            weights[f"in{l}"] = w_in[l]
            weights[f"out{l}"] = w_out[l]
            weights[f"ffn{l}"] = (w_gate[l], w_up[l])
            weights[f"down{l}"] = w_down[l]
        weights["in2"] = w_in_2[0]
        weights["branch2"] = w_branch_2[0]
        weights["out2"] = w_out_2[0]
        weights["ffn2"] = (w_ffn_gate_2[0], w_ffn_up_2[0])
        weights["down2"] = w_ffn_down_2[0]

        def is_down(stage):
            return stage.startswith("down")

        def is_ffn(stage):
            return stage.startswith("ffn")

        def lap_subs(stage, lap3):
            return DOWN_SUBS[4 * lap3:4 * lap3 + 4] if is_down(stage) else [2] * 4

        items1 = []
        for h in range(4):
            cols = slice(h * P, (h + 1) * P)
            items1 += [(QA[:, :, cols], P, QAT[:, h, :], HD ** -0.5), (KA[:, :, cols], P, KAT[:, h, :], 1.0)]
        for h in range(8):
            items1 += [(QB[:, :, h, :], 66, QBT[0:66, h, :], HD ** -0.5), (KB[:, :, h, :], 66, KBT[0:66, h, :], 1.0)]
        items2 = []
        for h in range(4):
            cols = slice(h * P, (h + 1) * P)
            items2 += [(QS[:, :, cols], P, QST[:, h, :], qkg[:, 0:1]), (KS[:, :, cols], P, KST[:, h, :], qkg[:, 1:2])]
        for h in range(4):
            cols = slice(h * P, (h + 1) * P)
            items2 += [(QH[:, :, cols], P, QHT[:, h, :], 1.0), (KEY[:, :, cols], P, KHT[:, h, :], 1.0)]
        units1 = [("diff", (h, m), i) for h in range(4) for i in range(T) for m in range(2)]
        units1 += [("fox", (h, 0), i) for h in range(8) for i in range(T)]
        units2 = [(h, j) for h in range(8) for j in reversed(range(T))]
        sp_at = {3: 0, 2: 128, 1: 384, 0: 768}
        hg_units = [(i, h) for i in range(T) for h in range(4)]
        psum_flat = PS[:, :, :].rearrange("p b c -> p (b c)")
        psum_e = psum_flat[:, 0:NE * P].rearrange("p (l t) -> p l t", t=P)
        psum_a = psum_flat[:, 3 * 512:3 * 512 + (LEVELS + 1) * P].rearrange("p (l t) -> p l t", t=P)
        G2 = G[:, :].rearrange("p (a b) -> p a b", b=CW)
        dtot = small[:, 3, 0:4]

        def states_before(u):
            return min(u, 4 * (T - 1))

        block = ctx.enter_context(nc.Block())

        @block.sync
        def _(sp):
            for t in range(T):
                sp.dma_start(X[:, t, :], x[0, t * P:(t + 1) * P, :]).then_inc(x_in, 16)

            def load_lap(stage, lap, chunk, lap3):
                row = 2 * P * 4 * lap3
                for r, subs in enumerate(lap_subs(stage, lap3)):
                    rows = slice(row, row + subs * P)
                    row += subs * P
                    if lap is not None:
                        sp.wait_ge(lo_ready, 4 * (lap - 1) + r + 1)
                    if is_ffn(stage):
                        gate, up = weights[stage]
                        half = CW // 2
                        sp.dma_start(raw[:, r, :, 0:half],
                                     gate[rows, bass.ds(chunk * half, half)].rearrange("(k p) n -> p k n", p=P)
                                     ).then_inc(raw_in[r], 16)
                        sp.dma_start(raw[:, r, :, half:CW],
                                     up[rows, bass.ds(chunk * half, half)].rearrange("(k p) n -> p k n", p=P)
                                     ).then_inc(up_in[r], 16)
                    else:
                        sp.dma_start(raw[:, r, 0:subs, :],
                                     weights[stage][rows, bass.ds(chunk * CW, CW)].rearrange("(k p) n -> p k n", p=P)
                                     ).then_inc(raw_in[r], 16)

            for stage, laps in STAGES:
                first = 0
                if stage == STAGES[0][0]:
                    load_lap(stage, None, 0, 0)
                    first = 1
                if is_down(stage):
                    with sp.Fori(0, 2) as chunk:
                        for lap3 in range(3):
                            load_lap(stage, LAP0[stage] + chunk * 3 + lap3, chunk, lap3)
                else:
                    with sp.Fori(first, laps) as chunk:
                        load_lap(stage, LAP0[stage] + chunk, chunk, 0)
            for n in range(2):
                sp.wait_ge(final_ready, n + 1)
                sp.dma_start(out[0, :, n * CW:(n + 1) * CW].rearrange("(t p) n -> p t n", p=P),
                             X[:, :, n * CW:(n + 1) * CW]).then_inc(out_done, 16)
            sp.wait_ge(out_done, 32)

        @block.gpsimd
        def _(pool):
            def lo_lap(stage, lap, lap3):
                for r, subs in enumerate(lap_subs(stage, lap3)):
                    pool.wait_ge(hi_ready, 4 * lap + r + 1)
                    nc.gpsimd.tensor_tensor(w_lo[:, r, 0:subs, :], raw[:, r, 0:subs, :],
                                            w_hi[:, r, 0:subs, :].bitcast(F32), ALU.subtract).then_inc(lo_ready, 1)

            for stage, laps in STAGES:
                if is_down(stage):
                    with pool.Fori(0, 2) as chunk:
                        for lap3 in range(3):
                            lo_lap(stage, LAP0[stage] + chunk * 3 + lap3, lap3)
                elif stage != "branch2":
                    with pool.Fori(0, laps) as chunk:
                        lo_lap(stage, LAP0[stage] + chunk, 0)
                else:
                    lo_lap(stage, LAP0[stage], 0)
                    for u in range(len(units2)):
                        pool.wait_ge(w_exp, u + 1)
                        diag = sb_l[:, u % 3, 0:P]
                        nc.gpsimd.tensor_tensor(diag, diag, SUMS[:, BEFORE, :], ALU.mult).then_inc(w_mask, 1)
                    for u, (i, h) in enumerate(hg_units):
                        pool.wait_ge(e_exp, u + 1)
                        if u >= 2:
                            pool.wait_ge(oh_mm, u - 1)
                        nc.gpsimd.tensor_tensor(
                            hg_k[u % 2], hg_e[u % 2][:, 1:NE, :],
                            KHT[:, h, i * P:(i + 1) * P].unsqueeze(1).to_broadcast([P, LEVELS + 1, P]),
                            ALU.mult).then_inc(ke_done, 1)
                    lo_lap(stage, LAP0[stage] + 1, 0)

        @block.scalar
        def _(act):
            steps = [0]
            roots = [0]

            def link(ins):
                steps[0] += 1
                ins.then_inc(act_step, 1)
                act.wait_ge(act_step, steps[0])

            def hi_lap(stage, lap, lap3=0, ffn_lap=None):
                for r, subs in enumerate(lap_subs(stage, lap3)):
                    act.wait_ge(raw_in[r], 16 * lap + 16)
                    if is_ffn(stage):
                        act.wait_ge(up_in[r], 16 * ffn_lap + 16)
                    if not (isinstance(lap, int) and lap == 0):
                        act.wait_ge(w_used, 4 * (lap - 1) + r + 1)
                    nc.scalar.activation(w_hi[:, r, 0:subs, :], raw[:, r, 0:subs, :], ACT.Copy).then_inc(hi_ready, 1)

            def hi_first(stage):
                hi_lap(stage, LAP0[stage], 0, FFN_SEEN.get(stage))

            def transposed_hi(stage, scale=True):
                ts = TS_OF[stage]
                for k in range(KD):
                    act.wait_ge(ts_mm, KD * ts + k + 1)
                    nc.scalar.activation(xt_hi[:, k, :], PS[:, 4 + k % 4, :], ACT.Copy,
                                         scale=gcol[:, ts, k:k + 1]).then_inc(ts_hi, 1)

            def first_root(n, count):
                link(nc.scalar.activation(small[:, 3, 0:n], small[:, 0, 0:n], ACT.Ln, scale=1.0 / count, bias=EPS))
                roots[0] += 1
                nc.scalar.activation(small[:, 1, 0:n], small[:, 3, 0:n], ACT.Exp, scale=-0.5).then_inc(y0_ready, 1)

            def norm_squares(n):
                for t in range(T):
                    if n == 0:
                        act.wait_ge(x_in, 16 * T)
                    else:
                        act.wait_ge(x_ready, 4 * (n - 1) + t + 1)
                    nc.scalar.activation(XN[:, t, :], X[:, t, :], ACT.Square,
                                         accum_out=small[:, 0, t:t + 1]).then_inc(sq_done, 1)
                act.wait_ge(sq_done, 4 * n + 4)
                first_root(T, D)

            def post_squares(stage, chunk, chunks_seen, junk):
                s = chunk % 2
                if chunk:
                    act.wait_ge(evac[0], SET0[stage][0] + 1)
                act.wait_ge(yg_done, chunks_seen + chunk + 1)
                for t in range(T):
                    last = nc.scalar.activation(junk[:, t, :], PS[:, 4 * s + t, :], ACT.Square,
                                                accum_out=ssq[:, chunk, t:t + 1])
                last.then_inc(evac[s], 1)

            for dst, src in ((ident[:, :], identity), (gcol[:, 0, :], attn_pre_g[0].rearrange("(k p) -> p k", p=P))):
                act.dma_start(dst, src, allow_slow_non_contiguous=True).then_inc(first_in, 16)
            loads = [
                (SUMS[:, :, :], sums), (causal_f, causal), (pairs_f, pairs),
                (pos_i, positions[0].rearrange("(t p) -> p t", p=P)), (freq, inv_freq.partition_broadcast(P)),
                (gcol[:, 3, :], attn_pre_g[1].rearrange("(k p) -> p k", p=P)),
                (gcol[:, 6, :], norm1_g_2[0].rearrange("(k p) -> p k", p=P)),
                (gcol[:, 9, :], norm2_g_2[0].rearrange("(k p) -> p k", p=P)),
                (gcol[:, 7, 4:5], hg_norm_g_2[0].unsqueeze(1)),
            ]
            for l in range(DEPTH):
                loads += [
                    (fw_raw[:, l], w_in[l][:, 3072:3080].rearrange("(k p) n -> p k n", p=P)),
                    (fbias[:, l, :], forget_bias[l].partition_broadcast(P)),
                    (gcol[:, 3 * l + 2, :], ffn_pre_g[l].rearrange("(k p) -> p k", p=P)),
                    (gcol[:, 3 * l + 1, 0:1], diff_sub_g[l].unsqueeze(1)),
                ]
                for n, v in enumerate((lam_q1, lam_k1, lam_q2, lam_k2)):
                    loads.append((lam_in[:, 4 * l + n, :], v[l].partition_broadcast(P)))
            for n in range(2):
                loads.append((qkg[64 * n:64 * n + 64, 0:1], q_norm_g_2[0].unsqueeze(1)))
                loads.append((qkg[64 * n:64 * n + 64, 1:2], k_norm_g_2[0].unsqueeze(1)))
            for dst, src in loads:
                act.dma_start(dst, src, allow_slow_non_contiguous=True).then_inc(const_in, 16)
            const_total.append(16 * len(loads))
            act.dma_start(G[:, :], attn_post_g[0].partition_broadcast(P)).then_inc(gain_in, 16)
            act.preload_act_table_set(EXP_TABLE)

            norm_squares(0)
            hi_lap("in0", 0)
            act.wait_ge(first_in, 32)
            transposed_hi("in0")

            act.wait_ge(lam_dots, 1)
            nc.scalar.activation(lam_s[:, 4:8], lam_s[:, 0:4], ACT.Exp).then_inc(lam_exps, 1)
            act.preload_act_table(ACT.Sin)
            nc.scalar.activation(cs[:, :, :, :], ang[:, 4:6], ACT.Sin).then_inc(trig_done, 1)
            act.preload_act_table_set(EXP_TABLE)

            def attention1(l):
                stage = f"in{l}"
                with act.Fori(0, LAPS[stage] - 1) as i:
                    hi_lap(stage, LAP0[stage] + 1 + i)
                hi_first(f"out{l}")
                act.wait_ge(f_biased, l + 1)
                link(nc.scalar.activation(fy[:, 1], fy[:, 0], ACT.Abs))
                link(nc.scalar.activation(fy[:, 1], fy[:, 1], ACT.Exp, scale=-1.0))
                nc.scalar.activation(fy[:, 1], fy[:, 1], ACT.Ln, bias=1.0).then_inc(f_log, 1)
                for n, (src, rows, dst, scale) in enumerate(items1):
                    if n % 2 == 0:
                        act.wait_ge(tr_mm, len(items1) * l + n + 1)
                        nc.scalar.activation(dst, PS[0:rows, 2 + n % 6, :], ACT.Copy, scale=scale).then_inc(tr_act, 1)
                b = len(units1) * l
                for u in range(len(units1) + 1):
                    if u < len(units1):
                        i = units1[u][2]
                        act.wait_ge(max_done, b + u + 1)
                        if b + u >= 2:
                            act.wait_ge(pt_mm, b + u - 1)
                        nc.scalar.activation(prob[:, u % 2, 0:P * (i + 1)], PS[:, u % 2, 0:P * (i + 1)], ACT.Exp,
                                             bias=nmax[:, u % 4:u % 4 + 1]).then_inc(exp_done, 1)
                    if u >= 1:
                        v = u - 1
                        i = units1[v][2]
                        act.wait_ge(pt_mm, b + v + 1)
                        if b + v >= 2:
                            act.wait_ge(o_mm, b + v - 1)
                        nc.scalar.activation(probT[:, v % 2, 0:P * (i + 1)], PS[:, 2 + v % 2, 0:P * (i + 1)],
                                             ACT.Copy).then_inc(pt_ev, 1)
                act.wait_ge(ss_ready, 3 * l + 1)
                first_root(16, 2 * HD)

            def product_with_post(stage, n_post, next_stage, junk):
                laps = LAPS[stage] // 2
                for chunk in range(2):
                    for lap3 in range(laps):
                        lap = chunk * laps + lap3 + 1
                        if lap < LAPS[stage]:
                            hi_lap(stage, LAP0[stage] + lap, lap % laps)
                        else:
                            hi_first(next_stage)
                    post_squares(stage, chunk, 2 * n_post, junk)
                act.wait_ge(ss_ready, ss_after[stage])
                first_root(T, D)
                gains = {"out0": ffn_post_g[0], "down0": attn_post_g[1], "out1": ffn_post_g[1]}
                if stage in gains:
                    act.dma_start(G[:, :], gains[stage].partition_broadcast(P)).then_inc(gain_in, 16)
                if stage == "down1":
                    act.dma_start(lb_tmp[:, 0:2, :], lb_table_2.partition_broadcast(P)).then_inc(lb_in, 16)

            def swiglu(stage, next_stage):
                seen = FFN_SEEN[stage]
                act.preload_act_table(ACT.Silu)

                def chunk_body(c, s, last):
                    if last:
                        hi_first(next_stage)
                    else:
                        hi_lap(stage, LAP0[stage] + c + 1, 0, seen + c + 1)
                    act.wait_ge(w_used, 4 * (LAP0[stage] + c) + 4)
                    if not (isinstance(c, int) and seen + c == 0):
                        act.wait_ge(h_mul, 2 * (seen + c))
                    nc.scalar.activation(silu_g[:, :, :], PS[:, 4 * s:4 * s + 2, :], ACT.Silu).then_inc(silu_done, 1)

                chunk_body(0, 0, False)
                chunk_body(1, 1, False)
                with act.Fori(1, 5) as i:
                    chunk_body(2 * i, 0, False)
                    chunk_body(2 * i + 1, 1, False)
                chunk_body(10, 0, True)
                act.preload_act_table_set(EXP_TABLE)

            ss_after = {"out0": 2, "down0": 3, "out1": 5, "down1": 6}
            for l in range(DEPTH):
                attention1(l)
                transposed_hi(f"out{l}")
                product_with_post(f"out{l}", 2 * l, f"ffn{l}", SQ)
                norm_squares(2 * l + 1)
                transposed_hi(f"ffn{l}")
                swiglu(f"ffn{l}", f"down{l}")
                product_with_post(f"down{l}", 2 * l + 1, f"in{l + 1}", junk_down)
                if l == DEPTH - 1:
                    act.wait_ge(lb_max, 1)
                    nc.scalar.activation(lb_tmp[:, 0:2, :], lb_tmp[:, 0:2, :], ACT.Exp).then_inc(lb_exp, 1)
                norm_squares(2 * l + 2)
                transposed_hi(f"in{l + 1}")

            def in2_hi(c):
                if c + 1 < LAPS["in2"]:
                    hi_lap("in2", LAP0["in2"] + c + 1)
                else:
                    hi_first("branch2")

            def chunk_done(c):
                act.wait_ge(w_used, 4 * (LAP0["in2"] + c) + 4)

            for n in range(2):
                in2_hi(n)
                act.wait_ge(qk_copied, n + 1)
                nc.scalar.activation(SQ2, (QS, KS)[n], ACT.Square).then_inc(qk_sq, 1)
                act.wait_ge(ss_ready, 7 + n)
                first_root(32, HD)
            in2_hi(2)
            act.preload_act_table(ACT.Sigmoid)
            for c, dst in ((3, QH), (4, KEY), (6, GG)):
                in2_hi(c)
                chunk_done(c)
                ins = nc.scalar.activation(dst, PS[:, 4 * (c % 2):4 * (c % 2) + 4, :], ACT.Sigmoid)
                ins.then_inc(sig_done, 1)
                if c == 4:
                    in2_hi(5)
            for c in range(7, 11):
                in2_hi(c)
                chunk_done(c)
                dst = (GATE_SB, GATE_HG)[(c - 7) // 2][:, :, ((c - 7) % 2) * CW:((c - 7) % 2 + 1) * CW]
                nc.scalar.activation(dst, PS[:, 4 * (c % 2):4 * (c % 2) + 4, :], ACT.Sigmoid).then_inc(evac[c % 2], 1)
            act.preload_act_table_set(EXP_TABLE)
            act.wait_ge(f_sum, 1)
            nc.scalar.activation(LOGF, LOGF, ACT.Ln).then_inc(log_done, 1)
            for n, (src, rows, dst, scale) in enumerate(items2):
                if n % 2 == 0:
                    act.wait_ge(tr_mm, 2 * len(items1) + n + 1)
                    nc.scalar.activation(dst, PS[:, n % 8, :], ACT.Copy, scale=scale).then_inc(tr_act, 1)

            for u in range(len(units2) + 1):
                if u < len(units2):
                    h, j = units2[u]
                    n = SEQ - P * j
                    buf = sb_l[:, u % 3, 0:n]
                    act.wait_ge(z_mm, u + 1)
                    if u >= 3:
                        act.wait_ge(av_mm, u - 2)
                    link(nc.scalar.activation(buf, PS[:, u % 2, 0:n], ACT.Abs))
                    link(nc.scalar.activation(buf, buf, ACT.Exp, scale=-1.0))
                    nc.scalar.activation(buf, buf, ACT.Ln, bias=1.0).then_inc(l_done, 1)
                if u >= 1:
                    h, j = units2[u - 1]
                    n = SEQ - P * j
                    buf = sb_l[:, (u - 1) % 3, 0:n]
                    act.wait_ge(arg_done, u)
                    nc.scalar.activation(buf, buf, ACT.Exp).then_inc(w_exp, 1)

            for u in range(len(hg_units) + 2):
                if u < len(hg_units):
                    act.wait_ge(e_mm, u + 1)
                    if u >= 2:
                        act.wait_ge(qe_done, u - 1)
                        act.wait_ge(ke_done, u - 1)
                    nc.scalar.activation(hg_e[u % 2], psum_e, ACT.Exp).then_inc(e_exp, 1)
                v = u - 1
                if 0 <= v < len(hg_units) and hg_units[v][0] < T - 1:
                    act.wait_ge(ket_mm, v + 1)
                    if v >= 2:
                        act.wait_ge(kv_mm, v - 1)
                    nc.scalar.activation(hg_ket[:, v % 2, :], PS[:, 5, 0:P], ACT.Copy).then_inc(ket_ev, 1)
                v = u - 2
                if v >= 0:
                    i, h = hg_units[v]
                    act.wait_ge(oh_mm, v + 1)
                    nc.scalar.activation(MIX[:, i, CW + h * P:CW + (h + 1) * P], PS[:, 6, 0:P], ACT.Copy).then_inc(oh_ev, 1)
            act.wait_ge(oh_ev, T * 4)
            nc.scalar.activation(SQ3, MIX[:, :, CW:D], ACT.Square).then_inc(sq_ready, 1)
            act.wait_ge(ss_ready, 9)
            first_root(16, P)
            transposed_hi("branch2")
            hi_lap("branch2", LAP0["branch2"] + 1)
            hi_first("out2")
            transposed_hi("out2")
            hi_lap("out2", LAP0["out2"] + 1)
            hi_first("ffn2")
            norm_squares(5)
            transposed_hi("ffn2")
            swiglu("ffn2", "down2")
            for lap in range(1, LAPS["down2"]):
                hi_lap("down2", LAP0["down2"] + lap, lap % 3)

        @block.vector
        def _(dve):
            V = nc.vector
            steps = [0]
            roots = [0]

            def link(ins):
                steps[0] += 1
                ins.then_inc(dve_step, 1)
                dve.wait_ge(dve_step, steps[0])

            def root(n, count):
                link(V.tensor_scalar(small[:, 2, 0:n], small[:, 0, 0:n], 1.0 / count, EPS, ALU.mult, ALU.add))
                roots[0] += 1
                dve.wait_ge(y0_ready, roots[0])
                link(V.tensor_tensor(small[:, 4, 0:n], small[:, 1, 0:n], small[:, 1, 0:n], ALU.mult))
                link(V.tensor_tensor(small[:, 4, 0:n], small[:, 4, 0:n], small[:, 2, 0:n], ALU.mult))
                link(V.tensor_scalar(small[:, 4, 0:n], small[:, 4, 0:n], -0.5, 1.5, ALU.mult, ALU.add))
                link(V.tensor_tensor(small[:, 5, 0:n], small[:, 1, 0:n], small[:, 4, 0:n], ALU.mult))

            def norm_scale(n):
                dve.wait_ge(sq_done, 4 * n + 4)
                root(T, D)
                for t in range(T):
                    V.tensor_scalar(XN[:, t, :], X[:, t, :], small[:, 5, t:t + 1], None, ALU.mult).then_inc(xn_ready, 1)

            def transposed_lo(stage):
                ts = TS_OF[stage]
                for k in range(KD):
                    dve.wait_ge(ts_hi, KD * ts + k + 1)
                    V.scalar_tensor_tensor(xt_lo[:, k, :], PS[:, 4 + k % 4, :], gcol[:, ts, k:k + 1],
                                           xt_hi[:, k, :].bitcast(F32), ALU.mult, ALU.subtract).then_inc(ts_lo, 1)

            def chunk_done(stage, lap):
                dve.wait_ge(w_used, 4 * (LAP0[stage] + lap) + 4)

            def banks(s):
                return PS[:, 4 * s:4 * s + 4, :]

            def heads(ap, n):
                return ap.rearrange("p t (h d) -> p t h d", h=n)

            norm_scale(0)
            dve.wait_ge(first_in, 32)
            transposed_lo("in0")

            dve.wait_ge(const_in, const_total[0])
            V.memset(gcol[:, 8, :], 1.0)
            for l in range(DEPTH):
                V.memset(gcol[:, 3 * l + 1, 4:8], 1.0)
            V.memset(gcol[:, 7, 0:4], 1.0)
            V.tensor_copy(ident_b[:, :], ident[:, :])
            V.tensor_copy(causal_b[:, :], causal_f)
            V.tensor_copy(PAIRS[:, :, :], pairs_f)
            V.tensor_copy(gcol[:, 7, 5:8], gcol[:, 7, 4:5].to_broadcast([P, 3]))
            for l in range(DEPTH):
                link(V.tensor_scalar(gcol[:, 3 * l + 1, 0:1], gcol[:, 3 * l + 1, 0:1], 1.0 - LAM_INIT[l], None, ALU.mult))
                V.tensor_copy(gcol[:, 3 * l + 1, 1:4], gcol[:, 3 * l + 1, 0:1].to_broadcast([P, 3]))
            V.tensor_scalar(qkg[:, 0:1], qkg[:, 0:1], HD ** -0.5, None, ALU.mult)
            link(V.tensor_copy(fw_hi[:, :, :, :], fw_raw))
            V.tensor_tensor(fw_lo[:, :, :, :], fw_raw, fw_hi[:, :, :, :].bitcast(F32), ALU.subtract).then_inc(fw_done, 1)
            link(V.tensor_copy(ang[:, 0, :, 0], pos_i))
            link(V.tensor_tensor(ang[:, 1], ang[:, 0, :, 0:1].to_broadcast([P, T, ROT]),
                                 freq.unsqueeze(1).to_broadcast([P, T, ROT]), ALU.mult))
            for n, quarter in ((0, 0.25), (1, 0.0)):
                link(V.tensor_scalar(ang[:, 2], ang[:, 1], 1.0 / (2 * math.pi), quarter, ALU.mult, ALU.add))
                link(V.tensor_scalar(ang[:, 3], ang[:, 2], ROUND, None, ALU.add))
                link(V.tensor_scalar(ang[:, 2], ang[:, 3], ROUND, None, ALU.subtract))
                link(V.scalar_tensor_tensor(ang[:, 4 + n], ang[:, 2], -TWO_PI[0], ang[:, 1], ALU.mult, ALU.add))
                for part in TWO_PI[1:]:
                    link(V.scalar_tensor_tensor(ang[:, 4 + n], ang[:, 2], -part, ang[:, 4 + n], ALU.mult, ALU.add))
                if quarter:
                    link(V.tensor_scalar(ang[:, 4 + n], ang[:, 4 + n], math.pi / 2, None, ALU.add))
                link(V.tensor_scalar(ang[:, 4 + n], ang[:, 4 + n], PI_F32, -PI_F32, ALU.min, ALU.max))
            q_k = lam_in.rearrange("p (a b) d -> p a b d", b=2)
            link(V.tensor_tensor(lam_t, q_k[:, :, 0, :], q_k[:, :, 1, :], ALU.mult))
            V.tensor_reduce(lam_s[:, 0:4], lam_t, AX.X, ALU.add).then_inc(lam_dots, 1)
            dve.wait_ge(lam_exps, 1)
            for l in range(DEPTH):
                link(V.tensor_tensor(lam[:, l:l + 1], lam_s[:, 4 + 2 * l:5 + 2 * l], lam_s[:, 5 + 2 * l:6 + 2 * l], ALU.subtract))
                link(V.tensor_scalar(lam[:, l:l + 1], lam[:, l:l + 1], LAM_INIT[l], -1.0, ALU.add, ALU.mult))

            def rotary(buf):
                b = heads(buf, 8)
                t1, t2 = b[:, :, :, 0:ROT], b[:, :, :, ROT:2 * ROT]
                cos, sin = (cs[:, n].unsqueeze(2).to_broadcast([P, T, 8, ROT]) for n in range(2))
                r = [rot[:, n].rearrange("p t (h d) -> p t h d", h=8) for n in range(4)]
                V.tensor_tensor(r[0], t1, cos, ALU.mult)
                V.tensor_tensor(r[1], t2, sin, ALU.mult)
                V.tensor_tensor(r[2], t2, cos, ALU.mult)
                link(V.tensor_tensor(r[3], t1, sin, ALU.mult))
                V.tensor_tensor(t1, r[0], r[1], ALU.subtract)
                link(V.tensor_tensor(t2, r[2], r[3], ALU.add))

            def attention1(l):
                stage = f"in{l}"
                dst = (QA, KA, None, QB[:, :, :, 0:HD], KB[:, :, :, 0:HD], VB[:, :, :, 0:HD])
                for c in range(6):
                    chunk_done(stage, c)
                    src = banks(c % 2)
                    if c == 2:
                        V.tensor_copy(VA[:, :, :, 0:P], heads(src, 4)).then_inc(evac[0], 1)
                    elif c > 2:
                        V.tensor_copy(dst[c], heads(src, 8)).then_inc(evac[c % 2], 1)
                    else:
                        link(V.tensor_copy(dst[c], src))
                        V.memset(mark[:, c:c + 1], 1.0).then_inc(evac[c % 2], 1)
                        if l == 0 and c == 0:
                            dve.wait_ge(trig_done, 1)
                        rotary(dst[c])
                V.memset(VA[:, :, :, P:P + 1], 1.0)
                V.memset(VB[:, :, :, HD:HD + 1], 1.0)
                V.memset(QB[:, :, :, 65:66], 8.0)
                V.memset(KB[:, :, :, 64:65], 1.0).then_inc(qkv_done, 1)
                dve.wait_ge(f_mm, l + 1)
                V.tensor_tensor(fy[:, 0], PS[:, 0, 0:T * 8].rearrange("p (t h) -> p t h", h=8),
                                fbias[:, l, :].unsqueeze(1).to_broadcast([P, T, 8]), ALU.add).then_inc(f_biased, 1)
                dve.wait_ge(f_log, l + 1)
                V.scalar_tensor_tensor(fy[:, 2], fy[:, 0], 0.0, fy[:, 1], ALU.min, ALU.subtract).then_inc(f_gate, 1)
                for n, (src, rows, to, scale) in enumerate(items1):
                    if n == 8:
                        dve.wait_ge(c_mm, l + 1)
                        c_sum = PS[:, 1, 0:T * 8].rearrange("p (t h) -> p t h", h=8)
                        V.tensor_scalar(QB[:, :, :, 64], c_sum, 8.0, None, ALU.mult)
                        V.tensor_scalar(KB[:, :, :, 65], c_sum, -1.0, None, ALU.mult).then_inc(c_placed, 1)
                    if n % 2:
                        dve.wait_ge(tr_mm, len(items1) * l + n + 1)
                        V.tensor_scalar(to, PS[0:rows, 2 + n % 6, :], scale, None, ALU.mult).then_inc(tr_dve, 1)
                b = len(units1) * l
                for u in range(len(units1) + 2):
                    if u < len(units1):
                        i = units1[u][2]
                        dve.wait_ge(s_mm, b + u + 1)
                        V.tensor_reduce(nmax[:, u % 4:u % 4 + 1], PS[:, u % 2, 0:P * (i + 1)], AX.X, ALU.max,
                                        negate=True).then_inc(max_done, 1)
                    if u >= 2:
                        v = u - 2
                        kind, (h, m), i = units1[v]
                        o = PS[:, 4 + v % 4, :]
                        r = rsum[:, v % 4:v % 4 + 1]
                        dve.wait_ge(o_mm, b + v + 1)
                        if kind == "fox":
                            link(V.reciprocal(r, o[:, HD:HD + 1]))
                            V.tensor_scalar(MIX[:, i, CW + h * HD:CW + (h + 1) * HD], o[:, 0:HD], r, None,
                                            ALU.mult).then_inc(o_norm, 1)
                        elif m == 0:
                            link(V.reciprocal(r, o[:, P:P + 1]))
                            V.tensor_scalar(otmp[:, i % 2, :], o[:, 0:P], r, None, ALU.mult).then_inc(o_norm, 1)
                        else:
                            link(V.reciprocal(r, o[:, P:P + 1]))
                            link(V.tensor_tensor(r, r, lam[:, l:l + 1], ALU.mult))
                            V.scalar_tensor_tensor(MIX[:, i, h * P:(h + 1) * P], o[:, 0:P], r, otmp[:, i % 2, :],
                                                   ALU.mult, ALU.add).then_inc(o_norm, 1)
                dve.wait_ge(o_norm, b + len(units1))
                mixed = MIX[:, :, 0:CW]
                link(V.tensor_tensor(SQ, mixed, mixed, ALU.mult))
                V.tensor_reduce(small[:, 0, 0:16].rearrange("p (t h) -> p t h", h=4), heads(SQ, 4), AX.X,
                                ALU.add).then_inc(ss_ready, 1)
                dve.wait_ge(ss_ready, 3 * l + 1)
                root(16, 2 * HD)
                for t in range(T):
                    row = MIX[:, t, 0:CW].rearrange("p (h d) -> p h d", h=4)
                    V.tensor_tensor(row, row, small[:, 5, 4 * t:4 * t + 4].unsqueeze(2).to_broadcast([P, 4, P]),
                                    ALU.mult).then_inc(xn_ready, 1)

            def product_with_post(stage, n_post, yg):
                laps = LAPS[stage] // 2
                for chunk in range(2):
                    cols = slice(chunk * CW, (chunk + 1) * CW)
                    chunk_done(stage, (chunk + 1) * laps - 1)
                    dve.wait_ge(gain_in, 16 * n_post + 16)
                    V.tensor_tensor(yg[:, :, cols], banks(chunk), G[:, cols].unsqueeze(1).to_broadcast([P, T, CW]),
                                    ALU.mult).then_inc(yg_done, 1)
                for s in range(2):
                    dve.wait_ge(evac[s], SET0[stage][s] + 1)
                V.tensor_tensor(small[:, 0, 0:T], ssq[:, 0, :], ssq[:, 1, :], ALU.add).then_inc(ss_ready, 1)
                dve.wait_ge(ss_ready, 3 * (n_post // 2) + n_post % 2 + 2)
                root(T, D)
                for t in range(T):
                    V.scalar_tensor_tensor(X[:, t, :], yg[:, t, :], small[:, 5, t:t + 1], X[:, t, :], ALU.mult,
                                           ALU.add).then_inc(x_ready, 1)

            def swiglu(stage):
                seen = FFN_SEEN[stage]

                def chunk_body(c, s):
                    dve.wait_ge(silu_done, seen + c + 1)
                    for j in range(2):
                        n = 2 * (seen + c) + j
                        if not (isinstance(n, int) and n == 0):
                            dve.wait_ge(h_lo, n)
                        V.tensor_tensor(h_tmp[:, :], silu_g[:, j, :], PS[:, 4 * s + 2 + j, :], ALU.mult).then_inc(h_mul, 1)
                        dve.wait_ge(h_mul, n + 1)
                        V.tensor_scalar(ht_hi[:, 2 * c + j, :], h_tmp[:, :], 1.0, None, ALU.mult).then_inc(h_hi, 1)
                        dve.wait_ge(h_hi, n + 1)
                        V.tensor_tensor(ht_lo[:, 2 * c + j, :], h_tmp[:, :], ht_hi[:, 2 * c + j, :].bitcast(F32),
                                        ALU.subtract).then_inc(h_lo, 1)

                chunk_body(0, 0)
                chunk_body(1, 1)
                with dve.Fori(1, 5) as i:
                    chunk_body(2 * i, 0)
                    chunk_body(2 * i + 1, 1)
                chunk_body(10, 0)

            for l in range(DEPTH):
                attention1(l)
                transposed_lo(f"out{l}")
                product_with_post(f"out{l}", 2 * l, YG_out)
                norm_scale(2 * l + 1)
                transposed_lo(f"ffn{l}")
                swiglu(f"ffn{l}")
                product_with_post(f"down{l}", 2 * l + 1, YG_down)
                if l == DEPTH - 1:
                    dve.wait_ge(lb_in, 16)
                    link(V.tensor_tensor(lb_tmp[:, 2, :], lb_tmp[:, 0, :], lb_tmp[:, 1, :], ALU.max))
                    V.tensor_tensor(lb_tmp[:, 0:2, :], lb_tmp[:, 0:2, :], lb_tmp[:, 2:3, :].to_broadcast([P, 2, CW]),
                                    ALU.subtract).then_inc(lb_max, 1)
                    dve.wait_ge(lb_exp, 1)
                    link(V.tensor_tensor(lb_tmp[:, 2, :], lb_tmp[:, 0, :], lb_tmp[:, 1, :], ALU.add))
                    link(V.reciprocal(lb_tmp[:, 3, :], lb_tmp[:, 2, :]))
                    link(V.tensor_tensor(G2[:, 0, :], lb_tmp[:, 0, :], lb_tmp[:, 3, :], ALU.mult))
                    link(V.tensor_scalar(G2[:, 1, :], G2[:, 0, :], -1.0, 1.0, ALU.mult, ALU.add))
                norm_scale(2 * l + 2)
                transposed_lo(f"in{l + 1}")

            for c in range(7):
                if c in (0, 1):
                    buf = (QS, KS)[c]
                    chunk_done("in2", c)
                    link(V.tensor_copy(buf, banks(c)))
                    V.memset(mark[:, c:c + 1], 1.0).then_inc(evac[c], 1)
                    V.memset(mark[:, 2:3], 1.0).then_inc(qk_copied, 1)
                    dve.wait_ge(qk_sq, c + 1)
                    V.tensor_reduce(small[:, 0, 0:32].rearrange("p (t h) -> p t h", h=8), heads(SQ2, 8), AX.X,
                                    ALU.add).then_inc(ss_ready, 1)
                    dve.wait_ge(ss_ready, 7 + c)
                    root(32, HD)
                    flat = buf.rearrange("p t (h d) -> p (t h) d", d=HD)
                    V.tensor_tensor(flat, flat, small[:, 5, 0:32].unsqueeze(2).to_broadcast([P, 32, HD]), ALU.mult)
                elif c in (2, 5):
                    chunk_done("in2", c)
                    V.tensor_copy((VS if c == 2 else VAL), banks(c % 2)).then_inc(evac[c % 2], 1)
                elif c in (3, 6):
                    buf = QH if c == 3 else GG
                    dve.wait_ge(sig_done, {3: 1, 6: 3}[c])
                    V.tensor_tensor(buf, buf, banks(c % 2), ALU.mult).then_inc(evac[c % 2], 1)
                else:
                    dve.wait_ge(sig_done, 2)
                    V.memset(mark[:, 3:4], 1.0).then_inc(evac[0], 1)
                    link(V.tensor_tensor(LOGF, KEY, G2[:, 1:2, :].to_broadcast([P, T, CW]), ALU.mult))
                    link(V.tensor_tensor(LOGF, LOGF, G2[:, 0:1, :].to_broadcast([P, T, CW]), ALU.add))
                    link(V.tensor_scalar(KEY, LOGF, -1.0, 1.0, ALU.mult, ALU.add))
                    V.tensor_scalar(LOGF, LOGF, 2.0 ** -62, None, ALU.max).then_inc(f_sum, 1)
            V.memset(mark[:, 2:3], 1.0).then_inc(qk2_done, 1)
            for n, (src, rows, to, scale) in enumerate(items2):
                if n % 2:
                    dve.wait_ge(tr_mm, 2 * len(items1) + n + 1)
                    V.tensor_scalar(to, PS[:, n % 8, :], scale, None, ALU.mult).then_inc(tr_dve, 1)

            for u in range(len(units2) + 3):
                if u < len(units2):
                    h, j = units2[u]
                    n = SEQ - P * j
                    z = PS[:, u % 2, 0:n]
                    lt = sb_l[:, u % 3, 0:n]
                    sp = sb_sp[:, h % 2, sp_at[j]:sp_at[j] + n]
                    dve.wait_ge(l_done, u + 1)
                    link(V.scalar_tensor_tensor(sp, z, 0.0, lt, ALU.max, ALU.add))
                    V.tensor_tensor(sp[:, 0:P], sp[:, 0:P], SUMS[:, BEFORE, :], ALU.mult)
                    V.scalar_tensor_tensor(lt, z, 0.0, lt, ALU.min, ALU.subtract).then_inc(sp_done, 1)
                if 1 <= u <= len(units2):
                    h, j = units2[u - 1]
                    n = SEQ - P * j
                    lt = sb_l[:, (u - 1) % 3, 0:n]
                    dve.wait_ge(rest_mm, u)
                    V.tensor_tensor(lt, lt, PS[:, 2 + (u - 1) % 2, 0:n], ALU.subtract).then_inc(arg_done, 1)
                if u >= 3 and units2[u - 3][1] == 0:
                    h = units2[u - 3][0]
                    dve.wait_ge(av_mm, u - 2)
                    V.tensor_copy(MIX[:, :, h * HD:(h + 1) * HD],
                                  PS[:, 4 + h % 2, 0:T * HD].rearrange("p (t d) -> p t d", d=HD)).then_inc(av_ev, 1)

            for u in range(len(hg_units) + 2):
                if u < len(hg_units):
                    i, h = hg_units[u]
                    dve.wait_ge(e_exp, u + 1)
                    if u >= 2:
                        dve.wait_ge(oh_mm, u - 1)
                    if i < T - 1:
                        V.tensor_copy(dtot[:, u % 4:u % 4 + 1], hg_e[u % 2][:, UPTO, P - 1:P])
                    V.tensor_tensor(hg_q[u % 2], hg_e[u % 2][:, 0:LEVELS + 1, :],
                                    QHT[:, h, i * P:(i + 1) * P].unsqueeze(1).to_broadcast([P, LEVELS + 1, P]),
                                    ALU.mult).then_inc(qe_done, 1)
                v = u - 1
                if 0 <= v < len(hg_units):
                    dve.wait_ge(a_mm, v + 1)
                    if v >= 1:
                        dve.wait_ge(a_sum, v)
                    V.tensor_tensor(hg_a, psum_a, PAIRS[:, :, :], ALU.mult).then_inc(a_read, 1)
                    dve.wait_ge(a_read, v + 1)
                    V.tensor_reduce(hg_at[:, v % 2, :], hg_a.rearrange("p l t -> p t l"), AX.X, ALU.add).then_inc(a_sum, 1)
                v = u - 2
                if v >= 0 and hg_units[v][0] < T - 1:
                    i, h = hg_units[v]
                    dve.wait_ge(kv_mm, v + 1)
                    dve.wait_ge(oh_mm, v + 1)
                    st = hg_state[:, h, :]
                    if i == 0:
                        V.tensor_copy(st, PS[:, 7, 0:P]).then_inc(state_done, 1)
                    else:
                        V.scalar_tensor_tensor(st, st, dtot[:, v % 4:v % 4 + 1], PS[:, 7, 0:P], ALU.mult,
                                               ALU.add).then_inc(state_done, 1)
            dve.wait_ge(sq_ready, 1)
            V.tensor_reduce(small[:, 0, 0:16].rearrange("p (t h) -> p t h", h=4), heads(SQ3, 4), AX.X,
                            ALU.add).then_inc(ss_ready, 1)
            dve.wait_ge(ss_ready, 9)
            root(16, P)
            for t in range(T):
                row = MIX[:, t, CW:D]
                rowh = row.rearrange("p (h d) -> p h d", h=4)
                link(V.tensor_tensor(rowh, rowh, small[:, 5, 4 * t:4 * t + 4].unsqueeze(2).to_broadcast([P, 4, P]), ALU.mult))
                V.tensor_tensor(row, row, GG[:, t, :], ALU.mult).then_inc(xn_ready, 1)
            transposed_lo("branch2")

            for q in range(4):
                cols = slice((q // 2) * CW, (q // 2 + 1) * CW)
                gate = (GATE_SB, GATE_HG)[q % 2][:, :, cols]
                dve.wait_ge(w_used, 4 * LAP0["branch2"] + 2 * q + 2)
                V.tensor_tensor(gate, gate, banks(q % 2), ALU.mult).then_inc(evac[q % 2], 1)
                if q % 2:
                    dve.wait_ge(evac[1], SET0["branch2"][1] + q // 2 + 1)
                    for t in range(T):
                        ins = V.tensor_tensor(GATE_SB[:, t, cols], GATE_SB[:, t, cols], GATE_HG[:, t, cols], ALU.add)
                        if q == 3:
                            ins.then_inc(xn_ready, 1)
            transposed_lo("out2")
            for n in range(2):
                cols = slice(n * CW, (n + 1) * CW)
                chunk_done("out2", n)
                for t in range(T):
                    ins = V.tensor_tensor(X[:, t, cols], X[:, t, cols], PS[:, 4 * n + t, :], ALU.add)
                    if n == 1:
                        ins.then_inc(x_ready, 1)
                if n == 0:
                    ins.then_inc(evac[0], 1)
            norm_scale(5)
            transposed_lo("ffn2")
            swiglu("ffn2")
            for n in range(2):
                cols = slice(n * CW, (n + 1) * CW)
                chunk_done("down2", 3 * n + 2)
                V.tensor_tensor(X[:, :, cols], X[:, :, cols], banks(n), ALU.add).then_inc(final_ready, 1)

        @block.tensor
        def _(pe):
            mm = nc.tensor.matmul

            def three(out_, a_hi, a_lo, b_hi, b_lo, start, stop):
                mm(out_, a_hi, b_hi, start=start, stop=False)
                mm(out_, a_hi, b_lo, start=False, stop=False)
                return mm(out_, a_lo, b_hi, start=False, stop=stop)

            def transposed(stage, src):
                ts = TS_OF[stage]
                if SET0[stage][1]:
                    pe.wait_ge(evac[1], SET0[stage][1])
                for k in range(KD):
                    if k >= 4:
                        pe.wait_ge(ts_lo, KD * ts + k - 3)
                    for t in range(T):
                        if k == 0:
                            pe.wait_ge(xn_ready, T * ts + t + 1)
                        last = nc.tensor.transpose(PS[:, 4 + k % 4, t * P:(t + 1) * P],
                                                   src[:, t, k * P:(k + 1) * P], ident[:, :])
                    last.then_inc(ts_mm, 1)

            def set_free(stage, c, s):
                n = SET0[stage][s] + c // 2 if isinstance(c, int) else SET0[stage][s] + c
                if not (isinstance(n, int) and n == 0):
                    pe.wait_ge(evac[s], n)

            def use_slot(r, sub, out_banks, a_hi, a_lo, start, stop):
                for t in range(T):
                    tok = slice(t * P, (t + 1) * P)
                    last = three(out_banks[:, t, :], a_hi[:, tok], a_lo[:, tok], w_hi[:, r, sub, :], w_lo[:, r, sub, :],
                                 start, stop)
                return last

            def token_chunk(stage, lap, s, laps, first):
                a_hi, a_lo = (ht_hi, ht_lo) if is_down(stage) else (xt_hi, xt_lo)
                kn = KF if is_down(stage) else KD
                k = 0
                for lap3 in range(laps):
                    for r, subs in enumerate(lap_subs(stage, lap3)):
                        pe.wait_ge(lo_ready, 4 * (lap + lap3) + r + 1)
                        for sub in range(subs):
                            if first and not is_down(stage):
                                pe.wait_ge(ts_lo, KD * TS_OF[stage] + k + 1)
                            last = use_slot(r, sub, PS[:, 4 * s:4 * s + 4, :], a_hi[:, k, :], a_lo[:, k, :],
                                            k == 0, k == kn - 1)
                            k += 1
                        last.then_inc(w_used, 1)

            def project(stage):
                n = LAPS[stage]
                for c in range(2):
                    set_free(stage, c, c)
                    token_chunk(stage, LAP0[stage] + c, c, 1, c == 0)
                with pe.Fori(1, n // 2) as i:
                    for s in range(2):
                        pe.wait_ge(evac[s], SET0[stage][s] + i)
                        token_chunk(stage, LAP0[stage] + 2 * i + s, s, 1, False)
                if n % 2:
                    set_free(stage, n - 1, 0)
                    token_chunk(stage, LAP0[stage] + n - 1, 0, 1, False)

            def two_chunks(stage):
                laps = LAPS[stage] // 2
                for c in range(2):
                    set_free(stage, c, c)
                    token_chunk(stage, LAP0[stage] + c * laps, c, laps, c == 0)

            def swiglu(stage):
                seen = FFN_SEEN[stage]

                def chunk(c, s, first):
                    if not (isinstance(c, int) and c < 2):
                        pe.wait_ge(h_mul, 2 * (seen + c) - 2)
                    elif c == 0:
                        pe.wait_ge(evac[0], SET0[stage][0])
                    for r in range(R):
                        pe.wait_ge(lo_ready, 4 * (LAP0[stage] + c) + r + 1)
                        for sub in range(2):
                            k = 2 * r + sub
                            if first:
                                pe.wait_ge(ts_lo, KD * TS_OF[stage] + k + 1)
                            for j in range(4):
                                cols = slice(j * P, (j + 1) * P)
                                last = three(PS[:, 4 * s + j, :], w_hi[:, r, sub, cols], w_lo[:, r, sub, cols],
                                             xt_hi[:, k, :], xt_lo[:, k, :], k == 0, k == KD - 1)
                        last.then_inc(w_used, 1)

                chunk(0, 0, True)
                chunk(1, 1, False)
                with pe.Fori(1, 5) as i:
                    chunk(2 * i, 0, False)
                    chunk(2 * i + 1, 1, False)
                chunk(10, 0, False)
                pe.wait_ge(h_lo, 2 * (seen + 11))

            def transpose_item(n, base, items, bank, reuse):
                src, rows, _, _ = items[n]
                m = n - reuse
                if m >= 0:
                    done = base // 2 + m // 2 + 1
                    pe.wait_ge(tr_dve if m % 2 else tr_act, done)
                for t in range(T):
                    last = nc.tensor.transpose(PS[0:rows, bank, t * P:(t + 1) * P], src[:, t, :], ident[:, :])
                last.then_inc(tr_mm, 1)

            def attention1(l):
                stage = f"in{l}"
                pe.wait_ge(evac[0], SET0[stage][0] + 3)
                pe.wait_ge(fw_done, 1)
                for t in range(T):
                    tok = slice(t * P, (t + 1) * P)
                    for k in range(KD):
                        last = three(PS[:, 0, 8 * t:8 * t + 8], xt_hi[:, k, tok], xt_lo[:, k, tok],
                                     fw_hi[:, l, k, :], fw_lo[:, l, k, :], k == 0, k == KD - 1)
                last.then_inc(f_mm, 1)
                pe.wait_ge(evac[1], SET0[stage][1] + 3)
                pe.wait_ge(qkv_done, l + 1)
                base = len(items1) * l
                for n in range(8):
                    transpose_item(n, base, items1, 2 + n % 6, 6)
                pe.wait_ge(f_gate, l + 1)
                for t in range(T):
                    for before in range(t + 1):
                        last = mm(PS[:, 1, 8 * t:8 * t + 8], SUMS[:, UPTO if before == t else ONES, :], fy[:, 2, before, :],
                                  start=before == 0, stop=before == t)
                last.then_inc(c_mm, 1)
                pe.wait_ge(c_placed, l + 1)
                for n in range(8, len(items1)):
                    transpose_item(n, base, items1, 2 + n % 6, 6)
                pe.wait_ge(tr_act, (base + len(items1)) // 2)
                pe.wait_ge(tr_dve, (base + len(items1)) // 2)
                b = len(units1) * l
                for u in range(len(units1) + 2):
                    if u < len(units1):
                        kind, (h, m), i = units1[u]
                        tok, upto = slice(i * P, (i + 1) * P), P * (i + 1)
                        if kind == "diff":
                            q, kk = QAT[64 * m:64 * m + 64, h, tok], KAT[64 * m:64 * m + 64, h, 0:upto]
                        else:
                            q, kk = QBT[0:66, h, tok], KBT[0:66, h, 0:upto]
                        if b + u >= 2:
                            pe.wait_ge(exp_done, b + u - 1)
                        mm(PS[:, u % 2, 0:upto], q, kk, start=True, stop=False)
                        mm(PS[:, u % 2, upto - P:upto], ident_b[:, :], causal_b[:, :], start=False, stop=True).then_inc(s_mm, 1)
                    v = u - 1
                    if 0 <= v < len(units1):
                        i = units1[v][2]
                        pe.wait_ge(exp_done, b + v + 1)
                        if b + v >= 2:
                            pe.wait_ge(pt_ev, b + v - 1)
                        for j in range(i + 1):
                            last = nc.tensor.transpose(PS[:, 2 + v % 2, j * P:(j + 1) * P],
                                                       prob[:, v % 2, j * P:(j + 1) * P], ident[:, :])
                        last.then_inc(pt_mm, 1)
                    v = u - 2
                    if v >= 0:
                        kind, (h, m), i = units1[v]
                        vals, width = (VA, P + 1) if kind == "diff" else (VB, HD + 1)
                        pe.wait_ge(pt_ev, b + v + 1)
                        if b + v >= 4:
                            pe.wait_ge(o_norm, b + v - 3)
                        for j in range(i + 1):
                            last = mm(PS[:, 4 + v % 4, 0:width], probT[:, v % 2, j * P:(j + 1) * P], vals[:, j, h, :],
                                      start=j == 0, stop=j == i)
                        last.then_inc(o_mm, 1)

            pe.wait_ge(first_in, 32)
            transposed("in0", XN)
            for l in range(DEPTH):
                project(f"in{l}")
                attention1(l)
                transposed(f"out{l}", MIX)
                two_chunks(f"out{l}")
                transposed(f"ffn{l}", XN)
                swiglu(f"ffn{l}")
                two_chunks(f"down{l}")
                transposed(f"in{l + 1}", XN)

            project("in2")
            pe.wait_ge(evac[0], SET0["branch2"][0])
            pe.wait_ge(evac[1], SET0["branch2"][1])
            pe.wait_ge(qk2_done, 1)
            for n in range(len(items2)):
                transpose_item(n, 2 * len(items1), items2, n % 8, 8)
            pe.wait_ge(tr_act, len(items1) + len(items2) // 2)
            pe.wait_ge(tr_dve, len(items1) + len(items2) // 2)
            for u in range(len(units2) + 2):
                if u < len(units2):
                    h, j = units2[u]
                    n = SEQ - P * j
                    rows = slice(64 * (h % 2), 64 * (h % 2) + 64)
                    if u >= 2:
                        pe.wait_ge(sp_done, u - 1)
                    mm(PS[:, u % 2, 0:n], KST[rows, h // 2, j * P:(j + 1) * P], QST[rows, h // 2, j * P:SEQ],
                       start=True, stop=True).then_inc(z_mm, 1)
                v = u - 1
                if 0 <= v < len(units2):
                    h, j = units2[v]
                    n = SEQ - P * j
                    pe.wait_ge(sp_done, v + 1)
                    if v >= 2:
                        pe.wait_ge(arg_done, v - 1)
                    for jj in range(j, T):
                        m = SEQ - P * jj
                        last = mm(PS[:, 2 + v % 2, n - m:n], SUMS[:, AFTER if jj == j else ONES, :],
                                  sb_sp[:, h % 2, sp_at[jj]:sp_at[jj] + m], start=jj == j, stop=jj == T - 1)
                    last.then_inc(rest_mm, 1)
                v = u - 2
                if v >= 0:
                    h, j = units2[v]
                    pe.wait_ge(w_mask, v + 1)
                    if j == T - 1 and h >= 2:
                        pe.wait_ge(av_ev, h - 1)
                    for i in range(j, T):
                        last = mm(PS[:, 4 + h % 2, i * HD:(i + 1) * HD], sb_l[:, v % 3, (i - j) * P:(i - j + 1) * P],
                                  VS[:, j, h * HD:(h + 1) * HD], start=j == T - 1, stop=j == 0, skip_group_check=True)
                    last.then_inc(av_mm, 1)
            pe.wait_ge(av_ev, 8)
            pe.wait_ge(log_done, 1)
            for u in range(len(hg_units) + 2):
                if u < len(hg_units):
                    i, h = hg_units[u]
                    if u >= 1:
                        pe.wait_ge(e_exp, u)
                    lf = LOGF[:, i, h * P:(h + 1) * P]
                    for bank in range(3):
                        w = min(4, NE - 4 * bank)
                        last = mm(PS[:, bank, 0:w * P], lf, SUMS[:, 4 * bank:4 * bank + w, :], start=True, stop=True)
                    last.then_inc(e_mm, 1)
                v = u - 1
                if 0 <= v < len(hg_units):
                    i, h = hg_units[v]
                    tok = slice(i * P, (i + 1) * P)
                    pe.wait_ge(qe_done, v + 1)
                    pe.wait_ge(ke_done, v + 1)
                    if v >= 1:
                        pe.wait_ge(a_read, v)
                    for l in range(LEVELS + 1):
                        kk = KHT[:, h, tok] if l == 0 else hg_k[v % 2][:, l - 1, :]
                        q = QHT[:, h, tok] if l == 0 else hg_q[v % 2][:, l, :]
                        last = mm(psum_a[:, l, :], kk, q, start=True, stop=True)
                    last.then_inc(a_mm, 1)
                    if i < T - 1:
                        if v >= 1:
                            pe.wait_ge(ket_ev, v)
                        nc.tensor.transpose(PS[:, 5, 0:P], hg_k[v % 2][:, LEVELS, :], ident[:, :]).then_inc(ket_mm, 1)
                v = u - 2
                if v >= 0:
                    i, h = hg_units[v]
                    val = VAL[:, i, h * P:(h + 1) * P]
                    if i < T - 1:
                        pe.wait_ge(ket_ev, v + 1)
                        if v >= 1:
                            pe.wait_ge(state_done, v)
                        mm(PS[:, 7, 0:P], hg_ket[:, v % 2, :], val, start=True, stop=True).then_inc(kv_mm, 1)
                    pe.wait_ge(a_sum, v + 1)
                    if v >= 1:
                        pe.wait_ge(oh_ev, v)
                    last = mm(PS[:, 6, 0:P], hg_at[:, v % 2, :], val, start=True, stop=i == 0)
                    if i > 0:
                        pe.wait_ge(state_done, 4 * (i - 1) + h + 1)
                        last = mm(PS[:, 6, 0:P], hg_q[v % 2][:, UPTO, :], hg_state[:, h, :], start=False, stop=True)
                    last.then_inc(oh_mm, 1)
            transposed("branch2", MIX)
            for q in range(4):
                half = q % 2
                set_free("branch2", q, half)
                for r in (2 * half, 2 * half + 1):
                    pe.wait_ge(lo_ready, 4 * (LAP0["branch2"] + q // 2) + r + 1)
                    for sub in range(2):
                        k = 2 * r + sub
                        if q < 2:
                            pe.wait_ge(ts_lo, KD * TS_OF["branch2"] + (k if q == 0 else KD - 1) + 1)
                        last = use_slot(r, sub, PS[:, 4 * half:4 * half + 4, :], xt_hi[:, k, :], xt_lo[:, k, :],
                                        k % 4 == 0, k % 4 == 3)
                    last.then_inc(w_used, 1)
            transposed("out2", GATE_SB)
            two_chunks("out2")
            transposed("ffn2", XN)
            swiglu("ffn2")
            two_chunks("down2")


_INS = ["x", "positions", "attn_pre_g", "w_in", "forget_bias", "lam_q1", "lam_k1", "lam_q2", "lam_k2", "diff_sub_g",
        "w_out", "attn_post_g", "ffn_pre_g", "w_gate", "w_up", "w_down", "ffn_post_g", "norm1_g_2", "w_in_2",
        "q_norm_g_2", "k_norm_g_2", "lb_table_2", "hg_norm_g_2", "w_branch_2", "w_out_2", "norm2_g_2",
        "w_ffn_gate_2", "w_ffn_up_2", "w_ffn_down_2"]


def kernel(**inputs):
    import concourse.bacc as bacc
    from concourse.bass_utils import run_bass_kernel_spmd

    nc = bacc.Bacc("TRN2", target_bir_lowering=False, num_devices=1)
    arrays, args = {}, []
    for name in _INS:
        arrays[f"in_{name}"] = np.ascontiguousarray(inputs[name])
    for name, table in shape_constants().items():
        arrays[f"in_{name}"] = np.ascontiguousarray(table)
    for name, a in arrays.items():
        args.append(nc.dram_tensor(name, a.shape, mybir.dt.from_np(a.dtype), kind="ExternalInput").ap())
    args.append(nc.dram_tensor("out_0", (1, SEQ, D), F32, kind="ExternalOutput").ap())
    build(nc, *args)
    r = run_bass_kernel_spmd(nc, [arrays], core_ids=[0])
    return r.results[0]["out_0"]
```

```python
import math
from contextlib import ExitStack

import numpy as np
import concourse.bass as bass
from concourse import mybir

F32 = mybir.dt.float32
F32R = mybir.dt.float32r
BF16 = mybir.dt.bfloat16
I32 = mybir.dt.int32
ALU = mybir.AluOpType
ACT = mybir.ActivationFunctionType
AX = mybir.AxisListType

P = 128
SEQ = 512
D = 1024
DEPTH = 2
T = SEQ // P
KD = D // P
CW = 512
F = 2816
KF = F // P
HD = 64
NEG = -1.0e30
EPS = 1e-6
ROT = 8
THETA = 500000.0
LAM_INIT = [0.8 - 0.6 * math.exp(-0.3 * l) for l in range(DEPTH)]
R = 4
JOIN, TURN, PRODUCT, OUTPUT = 2, 5, 6, 7
PROBS = TURN + 1
LEVELS = 7
EXP_TABLE = "natural_log_exp_and_others"

TWO_PI = []
_rest = 2 * math.pi
for _bits in (6, 6, 6):
    _e = math.floor(math.log2(_rest)) - _bits + 1
    _part = math.floor(_rest / 2.0 ** _e) * 2.0 ** _e
    TWO_PI.append(_part)
    _rest -= _part
TWO_PI.append(_rest)
PI_F32 = float(np.nextafter(np.float32(math.pi), np.float32(0)))
ROUND = 1.5 * 2 ** 23


def shape_constants():
    s = np.arange(P)[:, None]
    t = np.arange(P)[None, :]
    sums = [s <= t]
    pairs = [s == t]
    for level in range(LEVELS):
        h = 1 << level
        same = (s >> level) == (t >> level)
        right = ((t >> level) & 1) == 1
        sums.append(same & np.where(right, s <= t, s > t))
        pairs.append(right & (((s >> level) & 1) == 0) & ((s >> (level + 1)) == (t >> (level + 1))))
    sums += [s > t, s < t, s >= 0 * t]
    return {
        "identity": np.eye(P, dtype=np.float32),
        "causal": np.where(t > s, np.float32(NEG), np.float32(0)),
        "sums": np.stack(sums, 1).astype(np.float32),
        "pairs": np.stack(pairs, 1).astype(np.float32),
        "inv_freq": (1.0 / (np.float32(THETA) ** (np.arange(0, 2 * ROT, 2, dtype=np.float32) / np.float32(2 * ROT)))).astype(np.float32),
    }


UPTO = 0
AFTER = LEVELS + 1
BEFORE = LEVELS + 2
ONES = LEVELS + 3

STAGES = []
for _l in range(DEPTH):
    STAGES += [(f"in{_l}", 6), (f"out{_l}", 2), (f"ffn{_l}", 11), (f"down{_l}", 6)]
STAGES += [("in2", 11), ("branch2", 2), ("out2", 2), ("ffn2", 11), ("down2", 6)]
LAP0 = {}
_at = 0
for _name, _n in STAGES:
    LAP0[_name] = _at
    _at += _n
LAPS = dict(STAGES)
FFN_SEEN = {"ffn0": 0, "ffn1": 11, "ffn2": 22}
SETS = {"in": (3, 3), "out": (1, 1), "ffn": (0, 0), "down": (1, 1), "in2": (6, 5), "branch": (2, 2), "out2": (1, 0)}
SET0 = {}
_a, _b = 0, 0
for _name, _n in STAGES:
    SET0[_name] = (_a, _b)
    _k = SETS.get(_name) or SETS[_name[:-1]]
    _a, _b = _a + _k[0], _b + _k[1]
DOWN_SUBS = [2] * 7 + [1, 1] + [2] * 3
assert sum(DOWN_SUBS) == KF


def build(nc, x, positions, attn_pre_g, w_in, forget_bias, lam_q1, lam_k1, lam_q2, lam_k2, diff_sub_g,
          w_out, attn_post_g, ffn_pre_g, w_gate, w_up, w_down, ffn_post_g, norm1_g_2, w_in_2,
          q_norm_g_2, k_norm_g_2, lb_table_2, hg_norm_g_2, w_branch_2, w_out_2, norm2_g_2,
          w_ffn_gate_2, w_ffn_up_2, w_ffn_down_2, identity, causal, sums, pairs, inv_freq, out):
    ctx = ExitStack()
    with ctx:
        def sb(name, shape, dt=F32, scope=ctx):
            return scope.enter_context(nc.sbuf_tensor(name, shape, dt))

        def sem(name):
            return ctx.enter_context(nc.semaphore(name))

        X = sb("X", [P, T, D])
        raw = sb("raw", [P, R, 2, CW])
        w_hi = sb("w_hi", [P, R, 2, CW], F32R)
        w_lo = sb("w_lo", [P, R, 2, CW], F32R)
        SUMS = sb("SUMS", [P, LEVELS + 4, P])
        PAIRS = sb("PAIRS", [P, LEVELS + 1, P], BF16)
        ident = sb("ident", [P, P])
        ident_b = sb("ident_b", [P, P], BF16)
        causal_b = sb("causal_b", [P, P], BF16)
        G = sb("G", [P, D])
        gcol = sb("gcol", [P, 10, KD])
        qkg = sb("qkg", [P, 2])
        cs = sb("cs", [P, 2, T, ROT])
        fw = sb("fw", [P, DEPTH, KD, 16], F32R)
        fbias = sb("fbias", [P, DEPTH, 8])
        lam = sb("lam", [P, DEPTH])
        small = sb("small", [P, 6, 32])
        ssq = sb("ssq", [P, 2, T])
        vbase = sb("vbase", [P, T])
        nmax = sb("nmax", [P, 4])
        rsum = sb("rsum", [P, 4])
        dsum = sb("dsum", [P, 8, 2])
        drec = sb("drec", [P, 8, 2])
        mixc = sb("mixc", [P, 8])
        mark = sb("mark", [P, 4])
        fy = sb("fy", [P, 3, T, 8])

        r1 = ExitStack()
        xt_hi = sb("xt_hi", [P, KD, SEQ], F32R, r1)
        xt_lo = sb("xt_lo", [P, KD, SEQ], F32R, r1)
        r1.close()
        R1 = sb("R1", [P, 2 * KD * SEQ])
        r2 = ExitStack()
        ht_hi = sb("ht_hi", [P, KF, SEQ], F32R, r2)
        ht_lo = sb("ht_lo", [P, KF, SEQ], F32R, r2)
        silu_g = sb("silu_g", [P, 2, SEQ], F32, r2)
        h_tmp = sb("h_tmp", [P, SEQ], F32, r2)
        r2.close()
        R2 = sb("R2", [P, 24576])

        def at1(a, *dims):
            return view(R1, a, dims)

        def at2(a, *dims):
            return view(R2, a, dims)

        def view(tensor, a, dims):
            n = int(np.prod(dims))
            ap = tensor[:, a:a + n]
            if len(dims) == 2:
                return ap.rearrange("p (a b) -> p a b", b=dims[1])
            if len(dims) == 3:
                return ap.rearrange("p (a b c) -> p a b c", b=dims[1], c=dims[2])
            return ap

        XN = at2(0, T, D)
        QA = at2(0, T, CW)
        KA = at2(2048, T, CW)
        MIX = XN
        VA = at2(4096, T, CW)
        QB = at2(6160, T, 8, 66)
        KB = at2(8272, T, 8, 66)
        VB = at2(10384, T, 8, 65)
        QAT = at2(12464, 4, SEQ)
        KAT = at2(14512, 4, SEQ)
        prob = at2(16560, PROBS, SEQ)
        probT = at2(20144, 2, SEQ)
        f_rows = at2(21168, 1, SEQ)[0:16, 0, :]
        SQ = at2(21168, T, CW)
        rot = at2(16560, 4, T, ROT * 8)
        QBT = at1(0, 8, SEQ)
        KBT = at1(4096, 8, SEQ)
        YG_out = at2(4096, T, D)
        YG_down = at1(0, T, D)
        junk_down = at1(4096, T, CW)
        SQ2 = at2(20480, T, CW)
        QS, KS, VS = at2(0, T, CW), at2(2048, T, CW), at2(4096, T, CW)
        QH, KEY, LOGF, VAL, GG = (at2(6144 + 2048 * n, T, CW) for n in range(5))
        GATE_SB, GATE_HG = at2(16384, T, D), at2(20480, T, D)
        QST, KST, QHT, KHT = (at1(2048 * n, 4, SEQ) for n in range(4))
        sb_l = [at2(6144 + 512 * n, 1, SEQ)[:, 0, :] for n in range(3)] + [XN[:, n, CW:D] for n in range(3)]
        sb_sp = at2(7680, 2, 1280)
        NE = LEVELS + 2
        hg_e = (at1(0, NE, P), at1(NE * P, NE, P))
        hg_q = (at2(6144, LEVELS + 1, P), at2(7168, LEVELS + 1, P))
        hg_k = (at2(8192, LEVELS + 1, P), at2(9216, LEVELS + 1, P))
        hg_a = at2(4096, LEVELS + 1, P)
        hg_at = at2(5120, 2, P)
        hg_ket = at2(5376, 2, P)
        hg_state = at1(2 * NE * P, 4, P)
        SQ3 = at1(2 * NE * P + 4 * P, 4, P)
        lb_tmp = at2(20480, 4, CW)
        pos_i = at2(12000, T).bitcast(I32)
        ang = at2(12016, 8, T, ROT)
        freq = at2(12304, ROT)
        fw_raw = at2(12320, DEPTH, KD, 8)
        causal_f = at2(12448, P)
        pairs_f = at2(12576, LEVELS + 1, P)
        lam_in = at2(13600, DEPTH * 4, HD)
        lam_s = at2(14112, 8)
        lam_t = at2(14120, DEPTH * 2, HD)

        PS = ctx.enter_context(nc.psum_tensor("PS", [P, 8, 512], F32))

        x_in = [sem(f"x_in{t}") for t in range(T)]
        const_in = sem("const_in")
        gain_in = sem("gain_in")
        raw_in = [sem(f"raw_in{r}") for r in range(R)]
        up_in = [sem(f"up_in{r}") for r in range(R)]
        hi_ready, lo_ready, w_used = sem("hi_ready"), sem("lo_ready"), sem("w_used")
        evac = [sem("evac0"), sem("evac1")]
        xn_ready, ts_mm, ts_hi, ts_lo = sem("xn_ready"), sem("ts_mm"), sem("ts_hi"), sem("ts_lo")
        x_ready, sq_done, ss_ready, y0_ready = sem("x_ready"), sem("sq_done"), sem("ss_ready"), sem("y0_ready")
        yg_done, tile_done, half_sq, base_ready = (
            sem(n) for n in ("yg_done", "tile_done", "half_sq", "base_ready"))
        silu_done, h_mul, h_hi, h_lo = sem("silu_done"), sem("h_mul"), sem("h_hi"), sem("h_lo")
        trig_done, lam_dots, lam_exps = sem("trig_done"), sem("lam_dots"), sem("lam_exps")
        fw_done, first_in, lb_in = sem("fw_done"), sem("first_in"), sem("lb_in")
        dve_step, act_step = sem("dve_step"), sem("act_step")
        qk2_done = sem("qk2_done")
        f_mm, f_copied, f_turned, f_biased, f_log, f_gate, c_mm, c_placed = (sem(n) for n in ("f_mm", "f_copied", "f_turned", "f_biased", "f_log", "f_gate", "c_mm", "c_placed"))
        tr_mm, tr_act, tr_dve = sem("tr_mm"), sem("tr_act"), sem("tr_dve")
        s_mm, max_done, exp_done, pt_mm, pt_ev, o_mm, o_norm = (
            sem(n) for n in ("s_mm", "max_done", "exp_done", "pt_mm", "pt_ev", "o_mm", "o_norm"))
        out_done = sem("out_done")
        lb_max, lb_exp = sem("lb_max"), sem("lb_exp")
        sig_done, qk_copied, qk_sq, log_done, f_sum = (sem(n) for n in ("sig_done", "qk_copied", "qk_sq", "log_done", "f_sum"))
        z_mm, l_done, sp_done, rest_mm, arg_done, w_exp, w_mask, av_mm, av_ev = (
            sem(n) for n in ("z_mm", "l_done", "sp_done", "rest_mm", "arg_done", "w_exp", "w_mask", "av_mm", "av_ev"))
        e_mm, e_exp, qe_done, ke_done, a_mm, a_sum, ket_mm, ket_ev, kv_mm, state_done, oh_mm, oh_ev = (
            sem(n) for n in ("e_mm", "e_exp", "qe_done", "ke_done", "a_mm", "a_sum", "ket_mm", "ket_ev", "kv_mm",
                             "state_done", "oh_mm", "oh_ev"))
        a_read, joined, diff_sq, diff_rstd = sem("a_read"), sem("joined"), sem("diff_sq"), sem("diff_rstd")
        final_ready = sem("final_ready")

        const_total = []
        TS_OF = {"in0": 0, "out0": 1, "ffn0": 2, "in1": 3, "out1": 4, "ffn1": 5, "in2": 6, "branch2": 7, "out2": 8, "ffn2": 9}
        weights = {}
        for l in range(DEPTH):
            weights[f"in{l}"] = w_in[l]
            weights[f"out{l}"] = w_out[l]
            weights[f"ffn{l}"] = (w_gate[l], w_up[l])
            weights[f"down{l}"] = w_down[l]
        weights["in2"] = w_in_2[0]
        weights["branch2"] = w_branch_2[0]
        weights["out2"] = w_out_2[0]
        weights["ffn2"] = (w_ffn_gate_2[0], w_ffn_up_2[0])
        weights["down2"] = w_ffn_down_2[0]

        def is_down(stage):
            return stage.startswith("down")

        def first_set(stage):
            return 1 if is_down(stage) else 0

        def is_ffn(stage):
            return stage.startswith("ffn")

        TAIL = 1
        TILED = ["out0", "down0", "out1", "down1", "out2", "down2"]

        def wait_tile(engine, stage, t):
            if t < T - 1:
                engine.wait_ge(tile_done, (T - 1) * TILED.index(stage) + t + 1)
            else:
                engine.wait_ge(w_used, 4 * (LAP0[stage] + LAPS[stage]))

        DIFF_SUMS, DIFF_ROOT = 43, 49

        def lap_subs(stage, lap3):
            return DOWN_SUBS[4 * lap3:4 * lap3 + 4] if is_down(stage) else [2] * 4

        items1 = []
        for h in range(4):
            cols = slice(h * P, (h + 1) * P)
            items1 += [(QA[:, :, cols], P, QAT[:, h, :], HD ** -0.5), (KA[:, :, cols], P, KAT[:, h, :], 1.0)]
        for h in range(8):
            items1 += [(QB[:, :, h, :], 66, QBT[0:66, h, :], HD ** -0.5), (KB[:, :, h, :], 66, KBT[0:66, h, :], 1.0)]
        items2 = []
        for h in range(4):
            cols = slice(h * P, (h + 1) * P)
            items2 += [(QS[:, :, cols], P, QST[:, h, :], qkg[:, 0:1]), (KS[:, :, cols], P, KST[:, h, :], qkg[:, 1:2])]
        for h in range(4):
            cols = slice(h * P, (h + 1) * P)
            items2 += [(QH[:, :, cols], P, QHT[:, h, :], 1.0), (KEY[:, :, cols], P, KHT[:, h, :], 1.0)]
        units1 = [("diff", (h, m), i) for h in range(4) for i in range(T) for m in range(2)]
        units1 += [("fox", (h, 0), i) for h in range(8) for i in range(T)]
        has_output = [not (kind == "diff" and m == 0) for kind, (h, m), i in units1]

        def outputs(u):
            return sum(has_output[:u + 1])

        def joins(u):
            return sum(1 for kind, (h, m), i in units1[:u + 1] if kind == "diff" and m == 1)

        n_out, n_join = outputs(len(units1) - 1), joins(len(units1) - 1)
        units2 = [(h, j) for h in range(8) for j in reversed(range(T))]
        sp_at = {3: 0, 2: 128, 1: 384, 0: 768}
        hg_units = [(i, h) for i in range(T) for h in range(4)]
        psum_flat = PS[:, :, :].rearrange("p b c -> p (b c)")
        psum_e = psum_flat[:, 0:NE * P].rearrange("p (l t) -> p l t", t=P)
        psum_a = psum_flat[:, 3 * 512:3 * 512 + (LEVELS + 1) * P].rearrange("p (l t) -> p l t", t=P)
        G2 = G[:, :].rearrange("p (a b) -> p a b", b=CW)
        dtot = small[:, 4, 28:32]

        def states_before(u):
            return min(u, 4 * (T - 1))

        block = ctx.enter_context(nc.Block())

        @block.sync
        def _(sp):
            for t in range(T):
                sp.dma_start(X[:, t, :], x[0, t * P:(t + 1) * P, :]).then_inc(x_in[t], 16)

            def load_lap(stage, lap, chunk, lap3):
                row = P * sum(sum(lap_subs(stage, before)) for before in range(lap3))
                for r, subs in enumerate(lap_subs(stage, lap3)):
                    rows = slice(row, row + subs * P)
                    row += subs * P
                    if lap is not None:
                        sp.wait_ge(lo_ready, 4 * (lap - 1) + r + 1)
                    if is_ffn(stage):
                        gate, up = weights[stage]
                        half = CW // 2
                        sp.dma_start(raw[:, r, :, 0:half],
                                     gate[rows, bass.ds(chunk * half, half)].rearrange("(k p) n -> p k n", p=P)
                                     ).then_inc(raw_in[r], 16)
                        sp.dma_start(raw[:, r, :, half:CW],
                                     up[rows, bass.ds(chunk * half, half)].rearrange("(k p) n -> p k n", p=P)
                                     ).then_inc(up_in[r], 16)
                    else:
                        sp.dma_start(raw[:, r, 0:subs, :],
                                     weights[stage][rows, bass.ds(chunk * CW, CW)].rearrange("(k p) n -> p k n", p=P)
                                     ).then_inc(raw_in[r], 16)

            load_lap("in0", None, 0, 0)
            loads = [
                (SUMS[:, :, :], sums), (causal_f, causal), (pairs_f, pairs),
                (pos_i, positions[0].rearrange("(t p) -> p t", p=P)), (freq, inv_freq.partition_broadcast(P)),
                (gcol[:, 3, :], attn_pre_g[1].rearrange("(k p) -> p k", p=P)),
                (gcol[:, 6, :], norm1_g_2[0].rearrange("(k p) -> p k", p=P)),
                (gcol[:, 9, :], norm2_g_2[0].rearrange("(k p) -> p k", p=P)),
                (gcol[:, 7, 4:5], hg_norm_g_2[0].unsqueeze(1)),
            ]
            for l in range(DEPTH):
                loads += [
                    (fw_raw[:, l], w_in[l][:, 3072:3080].rearrange("(k p) n -> p k n", p=P)),
                    (fbias[:, l, :], forget_bias[l].partition_broadcast(P)),
                    (gcol[:, 3 * l + 2, :], ffn_pre_g[l].rearrange("(k p) -> p k", p=P)),
                    (gcol[:, 3 * l + 1, 0:1], diff_sub_g[l].unsqueeze(1)),
                ]
                for n, v in enumerate((lam_q1, lam_k1, lam_q2, lam_k2)):
                    loads.append((lam_in[:, 4 * l + n, :], v[l].partition_broadcast(P)))
            for n in range(2):
                loads.append((qkg[64 * n:64 * n + 64, 0:1], q_norm_g_2[0].unsqueeze(1)))
                loads.append((qkg[64 * n:64 * n + 64, 1:2], k_norm_g_2[0].unsqueeze(1)))
            for dst, src in loads:
                sp.dma_start(dst, src, allow_slow_non_contiguous=True).then_inc(const_in, 16)
            const_total.append(16 * len(loads))
            sp.dma_start(G[:, :], attn_post_g[0].partition_broadcast(P)).then_inc(gain_in, 16)
            for stage, laps in STAGES:
                first = 1 if stage == "in0" else 0
                if is_down(stage):
                    with sp.Fori(0, 2) as chunk:
                        for lap3 in range(3):
                            load_lap(stage, LAP0[stage] + chunk * 3 + lap3, chunk, lap3)
                else:
                    with sp.Fori(first, laps) as chunk:
                        load_lap(stage, LAP0[stage] + chunk, chunk, 0)
            sp.wait_ge(final_ready, 1)
            sp.dma_start(out[0, :, 0:CW].rearrange("(t p) n -> p t n", p=P), X[:, :, 0:CW]).then_inc(out_done, 16)
            for t in range(T):
                sp.wait_ge(final_ready, t + 2)
                sp.dma_start(out[0, t * P:(t + 1) * P, CW:D], X[:, t, CW:D]).then_inc(out_done, 16)
            sp.wait_ge(out_done, 16 * (T + 1))

        @block.gpsimd
        def _(pool):
            def lo_lap(stage, lap, lap3):
                for r, subs in enumerate(lap_subs(stage, lap3)):
                    pool.wait_ge(hi_ready, 4 * lap + r + 1)
                    nc.gpsimd.tensor_tensor(w_lo[:, r, 0:subs, :], raw[:, r, 0:subs, :],
                                            w_hi[:, r, 0:subs, :].bitcast(F32), ALU.subtract).then_inc(lo_ready, 1)

            for stage, laps in STAGES:
                if is_down(stage):
                    with pool.Fori(0, 2) as chunk:
                        for lap3 in range(3):
                            lo_lap(stage, LAP0[stage] + chunk * 3 + lap3, lap3)
                elif stage in ("out0", "out1"):
                    l = int(stage[-1])
                    lo_lap(stage, LAP0[stage], 0)
                    mixed = MIX[:, :, 0:CW]
                    pool.wait_ge(o_norm, n_out * l + n_join)
                    nc.gpsimd.tensor_tensor(SQ, mixed, mixed, ALU.mult).then_inc(diff_sq, 1)
                    pool.wait_ge(diff_rstd, l + 1)
                    for t in range(T):
                        row = MIX[:, t, 0:CW].rearrange("p (h d) -> p h d", h=4)
                        nc.gpsimd.tensor_tensor(row, row, small[:, 5, 4 * t:4 * t + 4].unsqueeze(2).to_broadcast([P, 4, P]),
                                                ALU.mult).then_inc(xn_ready, 1)
                    lo_lap(stage, LAP0[stage] + 1, 0)
                elif stage != "branch2":
                    with pool.Fori(0, laps) as chunk:
                        lo_lap(stage, LAP0[stage] + chunk, 0)
                else:
                    lo_lap(stage, LAP0[stage], 0)
                    for u in range(len(units2)):
                        pool.wait_ge(w_exp, u + 1)
                        diag = sb_l[u % 6][:, 0:P]
                        nc.gpsimd.tensor_tensor(diag, diag, SUMS[:, BEFORE, :], ALU.mult).then_inc(w_mask, 1)
                    for u, (i, h) in enumerate(hg_units):
                        pool.wait_ge(e_exp, u + 1)
                        if u >= 2:
                            pool.wait_ge(oh_mm, u - 1)
                        nc.gpsimd.tensor_tensor(
                            hg_k[u % 2], hg_e[u % 2][:, 1:NE, :],
                            KHT[:, h, i * P:(i + 1) * P].unsqueeze(1).to_broadcast([P, LEVELS + 1, P]),
                            ALU.mult).then_inc(ke_done, 1)
                    lo_lap(stage, LAP0[stage] + 1, 0)

        @block.scalar
        def _(act):
            steps = [0]
            roots = [0]

            def link(ins):
                steps[0] += 1
                ins.then_inc(act_step, 1)
                act.wait_ge(act_step, steps[0])

            def hi_lap(stage, lap, lap3=0, ffn_lap=None, slots=range(R)):
                for r in slots:
                    subs = lap_subs(stage, lap3)[r]
                    act.wait_ge(raw_in[r], 16 * lap + 16)
                    if is_ffn(stage):
                        act.wait_ge(up_in[r], 16 * ffn_lap + 16)
                    if not (isinstance(lap, int) and lap == 0):
                        act.wait_ge(w_used, 4 * (lap - 1) + r + 1)
                    nc.scalar.activation(w_hi[:, r, 0:subs, :], raw[:, r, 0:subs, :], ACT.Copy).then_inc(hi_ready, 1)

            def hi_first(stage, slots=range(R)):
                hi_lap(stage, LAP0[stage], 0, FFN_SEEN.get(stage), slots)

            def transposed_hi(stage, late=R):
                ts = TS_OF[stage]
                for k in range(KD):
                    if k >= 4 and late + k - 4 < R:
                        hi_first(stage, [late + k - 4])
                    act.wait_ge(ts_mm, KD * ts + k + 1)
                    nc.scalar.activation(xt_hi[:, k, :], PS[:, 4 + k % 4, :], ACT.Copy,
                                         scale=gcol[:, ts, k:k + 1]).then_inc(ts_hi, 1)

            def first_root(n, count):
                link(nc.scalar.activation(small[:, 3, 0:n], small[:, 0, 0:n], ACT.Ln, scale=1.0 / count, bias=EPS))
                roots[0] += 1
                nc.scalar.activation(small[:, 1, 0:n], small[:, 3, 0:n], ACT.Exp, scale=-0.5).then_inc(y0_ready, 1)

            def norm_tile(n, t):
                if n == 0:
                    act.wait_ge(x_in[t], 16)
                else:
                    act.wait_ge(x_ready, 4 * (n - 1) + t + 1)
                nc.scalar.activation(XN[:, t, :], X[:, t, :], ACT.Square,
                                     accum_out=small[:, 0, t:t + 1]).then_inc(sq_done, 1)
                act.wait_ge(sq_done, 4 * n + t + 1)
                link(nc.scalar.activation(small[:, 3, t:t + 1], small[:, 0, t:t + 1], ACT.Ln, scale=1.0 / D, bias=EPS))
                nc.scalar.activation(small[:, 1, t:t + 1], small[:, 3, t:t + 1], ACT.Exp, scale=-0.5).then_inc(y0_ready, 1)
                roots[0] += 1

            def post_tile(stage, n_post, t, junk):
                first = first_set(stage)
                wait_tile(act, stage, t)
                if t == 0:
                    act.wait_ge(evac[first], SET0[stage][first] + 1)
                nc.scalar.activation(junk[:, t, :], PS[:, 4 * (1 - first) + t, :], ACT.Square,
                                     accum_out=ssq[:, 1, t:t + 1]).then_inc(half_sq, 1)
                if t == 0:
                    act.wait_ge(base_ready, n_post + 1)
                act.wait_ge(half_sq, 4 * n_post + t + 1)
                link(nc.scalar.activation(small[:, 3, t:t + 1], ssq[:, 1, t:t + 1], ACT.Ln, scale=1.0 / D,
                                          bias=vbase[:, t:t + 1]))
                nc.scalar.activation(small[:, 1, t:t + 1], small[:, 3, t:t + 1], ACT.Exp, scale=-0.5).then_inc(y0_ready, 1)
                roots[0] += 1

            def norm_follows(n, before):
                for t in range(T + 1):
                    if t < T:
                        before(t)
                    if t >= 1:
                        norm_tile(n, t - 1)

            for dst, src in ((ident[:, :], identity), (gcol[:, 0, :], attn_pre_g[0].rearrange("(k p) -> p k", p=P))):
                act.dma_start(dst, src, allow_slow_non_contiguous=True).then_inc(first_in, 16)
            act.preload_act_table_set(EXP_TABLE)

            for t in range(T):
                norm_tile(0, t)
            act.wait_ge(first_in, 32)
            hi_first("in0", range(1))
            transposed_hi("in0", 1)

            hi_lap("in0", 1)
            act.wait_ge(lam_dots, 1)
            nc.scalar.activation(lam_s[:, 4:8], lam_s[:, 0:4], ACT.Exp).then_inc(lam_exps, 1)
            act.preload_act_table(ACT.Sin)
            nc.scalar.activation(cs[:, :, :, :], ang[:, 4:6], ACT.Sin).then_inc(trig_done, 1)
            act.preload_act_table_set(EXP_TABLE)

            def attention1(l):
                stage = f"in{l}"
                with act.Fori(2 if l == 0 else 1, LAPS[stage]) as lap:
                    hi_lap(stage, LAP0[stage] + lap)
                hi_first(f"out{l}")
                act.wait_ge(f_mm, l + 1)
                nc.scalar.activation(f_rows, PS[0:16, 0, :], ACT.Copy).then_inc(f_copied, 1)
                act.wait_ge(f_biased, l + 1)
                link(nc.scalar.activation(fy[:, 1], fy[:, 0], ACT.Abs))
                link(nc.scalar.activation(fy[:, 1], fy[:, 1], ACT.Exp, scale=-1.0))
                nc.scalar.activation(fy[:, 1], fy[:, 1], ACT.Ln, bias=1.0).then_inc(f_log, 1)
                for n, (src, rows, dst, scale) in enumerate(items1):
                    if n % 2 == 0:
                        act.wait_ge(tr_mm, len(items1) * l + n + 1)
                        nc.scalar.activation(dst, PS[0:rows, 2 + n % 6, :], ACT.Copy, scale=scale).then_inc(tr_act, 1)
                b, bo, bj = len(units1) * l, n_out * l, n_join * l
                for u in range(len(units1) + TURN):
                    v = u - TURN
                    if v >= 0 and has_output[v]:
                        i = units1[v][2]
                        n = outputs(v)
                        act.wait_ge(pt_mm, bo + n)
                        if bo + n > 2:
                            act.wait_ge(o_mm, bo + n - 2)
                        nc.scalar.activation(probT[:, n % 2, 0:P * (i + 1)], PS[:, 4 + n % 2, 0:P * (i + 1)],
                                             ACT.Copy).then_inc(pt_ev, 1)
                    if u < len(units1):
                        kind, (h, m), i = units1[u]
                        act.wait_ge(max_done, b + u + 1)
                        if u >= PROBS and has_output[u - PROBS]:
                            act.wait_ge(pt_mm, bo + outputs(u - PROBS))
                        elif u >= PROBS:
                            act.wait_ge(joined, bj + joins(u - PROBS + 1))
                        elif l and u == 0:
                            act.wait_ge(pt_mm, bo)
                        sums_to = dict(accum_out=dsum[:, (u // 2) % 8, m:m + 1]) if kind == "diff" else {}
                        nc.scalar.activation(prob[:, u % PROBS, 0:P * (i + 1)], PS[:, u % 4, 0:P * (i + 1)], ACT.Exp,
                                             bias=nmax[:, u % 4:u % 4 + 1], **sums_to).then_inc(exp_done, 1)
                    if u == DIFF_ROOT:
                        act.wait_ge(ss_ready, l + 1)
                        first_root(16, 2 * HD)

            def product_with_post(stage, n_post, next_stage, junk):
                laps, first = LAPS[stage] // 2, first_set(stage)
                for lap in range(1, laps + 1):
                    hi_lap(stage, LAP0[stage] + lap, lap % laps)
                act.wait_ge(yg_done, n_post + 1)
                for t in range(T):
                    last = nc.scalar.activation(junk[:, t, :], PS[:, 4 * first + t, :], ACT.Square,
                                                accum_out=ssq[:, 0, t:t + 1])
                last.then_inc(evac[first], 1)
                for lap in range(laps + 1, 2 * laps):
                    hi_lap(stage, LAP0[stage] + lap, lap % laps)
                hi_first(next_stage, range(TAIL))
                norm_follows(n_post + 1, lambda t: post_tile(stage, n_post, t, junk))
                gains = {"out0": ffn_post_g[0], "down0": attn_post_g[1], "out1": ffn_post_g[1]}
                if stage in gains:
                    act.dma_start(G[:, :], gains[stage].partition_broadcast(P)).then_inc(gain_in, 16)
                if stage == "down1":
                    act.dma_start(lb_tmp[:, 0:2, :], lb_table_2.partition_broadcast(P)).then_inc(lb_in, 16)

            def swiglu(stage, next_stage):
                seen = FFN_SEEN[stage]
                act.preload_act_table(ACT.Silu)

                def chunk_body(c, s, last):
                    if last:
                        hi_first(next_stage)
                    else:
                        hi_lap(stage, LAP0[stage] + c + 1, 0, seen + c + 1)
                    act.wait_ge(w_used, 4 * (LAP0[stage] + c) + 4)
                    if not (isinstance(c, int) and seen + c == 0):
                        act.wait_ge(h_mul, 2 * (seen + c))
                    nc.scalar.activation(silu_g[:, :, :], PS[:, 4 * s:4 * s + 2, :], ACT.Silu).then_inc(silu_done, 1)

                chunk_body(0, 0, False)
                chunk_body(1, 1, False)
                with act.Fori(1, 5) as i:
                    chunk_body(2 * i, 0, False)
                    chunk_body(2 * i + 1, 1, False)
                chunk_body(10, 0, True)
                act.preload_act_table_set(EXP_TABLE)

            for l in range(DEPTH):
                attention1(l)
                transposed_hi(f"out{l}")
                product_with_post(f"out{l}", 2 * l, f"ffn{l}", SQ)
                transposed_hi(f"ffn{l}", TAIL)
                swiglu(f"ffn{l}", f"down{l}")
                product_with_post(f"down{l}", 2 * l + 1, f"in{l + 1}", junk_down)
                transposed_hi(f"in{l + 1}", TAIL)
            act.wait_ge(lb_max, 1)
            nc.scalar.activation(lb_tmp[:, 0:2, :], lb_tmp[:, 0:2, :], ACT.Exp).then_inc(lb_exp, 1)

            def in2_hi(c):
                if c + 1 < LAPS["in2"]:
                    hi_lap("in2", LAP0["in2"] + c + 1)
                else:
                    hi_first("branch2")

            def chunk_done(c):
                act.wait_ge(w_used, 4 * (LAP0["in2"] + c) + 4)

            for n in range(2):
                in2_hi(n)
                act.wait_ge(qk_copied, n + 1)
                nc.scalar.activation(SQ2, (QS, KS)[n], ACT.Square).then_inc(qk_sq, 1)
                act.wait_ge(ss_ready, DEPTH + n + 1)
                first_root(32, HD)
            in2_hi(2)
            act.preload_act_table(ACT.Sigmoid)
            for c, dst in ((3, QH), (4, KEY), (6, GG)):
                in2_hi(c)
                chunk_done(c)
                ins = nc.scalar.activation(dst, PS[:, 4 * (c % 2):4 * (c % 2) + 4, :], ACT.Sigmoid)
                ins.then_inc(sig_done, 1)
                if c == 4:
                    in2_hi(5)
            for c in range(7, 11):
                in2_hi(c)
                chunk_done(c)
                dst = (GATE_SB, GATE_HG)[(c - 7) // 2][:, :, ((c - 7) % 2) * CW:((c - 7) % 2 + 1) * CW]
                nc.scalar.activation(dst, PS[:, 4 * (c % 2):4 * (c % 2) + 4, :], ACT.Sigmoid).then_inc(evac[c % 2], 1)
            act.preload_act_table_set(EXP_TABLE)
            act.wait_ge(f_sum, 1)
            nc.scalar.activation(LOGF, LOGF, ACT.Ln).then_inc(log_done, 1)
            for n, (src, rows, dst, scale) in enumerate(items2):
                if n % 2 == 0:
                    act.wait_ge(tr_mm, 2 * len(items1) + n + 1)
                    nc.scalar.activation(dst, PS[:, n % 8, :], ACT.Copy, scale=scale).then_inc(tr_act, 1)

            for u in range(len(units2) + 3):
                if u < len(units2):
                    h, j = units2[u]
                    n = SEQ - P * j
                    buf = sb_l[u % 6][:, 0:n]
                    act.wait_ge(z_mm, u + 1)
                    if u >= 6:
                        act.wait_ge(av_mm, u - 5)
                    link(nc.scalar.activation(buf, PS[:, u % 3, 0:n], ACT.Abs))
                    link(nc.scalar.activation(buf, buf, ACT.Exp, scale=-1.0))
                    nc.scalar.activation(buf, buf, ACT.Ln, bias=1.0).then_inc(l_done, 1)
                v = u - 3
                if v >= 0:
                    h, j = units2[v]
                    n = SEQ - P * j
                    buf = sb_l[v % 6][:, 0:n]
                    act.wait_ge(arg_done, v + 1)
                    nc.scalar.activation(buf, buf, ACT.Exp).then_inc(w_exp, 1)

            for u in range(len(hg_units) + 2):
                if u < len(hg_units):
                    act.wait_ge(e_mm, u + 1)
                    if u >= 2:
                        act.wait_ge(qe_done, u - 1)
                        act.wait_ge(ke_done, u - 1)
                    nc.scalar.activation(hg_e[u % 2], psum_e, ACT.Exp).then_inc(e_exp, 1)
                v = u - 1
                if 0 <= v < len(hg_units) and hg_units[v][0] < T - 1:
                    act.wait_ge(ket_mm, v + 1)
                    if v >= 2:
                        act.wait_ge(kv_mm, v - 1)
                    nc.scalar.activation(hg_ket[:, v % 2, :], PS[:, 5, 0:P], ACT.Copy).then_inc(ket_ev, 1)
                v = u - 2
                if v >= 0:
                    i, h = hg_units[v]
                    act.wait_ge(oh_mm, v + 1)
                    nc.scalar.activation(SQ3[:, h, :], PS[:, 6, 0:P], ACT.Square, accum_out=small[:, 0, v:v + 1])
                    nc.scalar.activation(MIX[:, i, CW + h * P:CW + (h + 1) * P], PS[:, 6, 0:P], ACT.Copy).then_inc(oh_ev, 1)
                    if h == 3:
                        act.wait_ge(oh_ev, v + 1)
                        cols = slice(4 * i, 4 * i + 4)
                        link(nc.scalar.activation(small[:, 3, cols], small[:, 0, cols], ACT.Ln, scale=1.0 / P, bias=EPS))
                        nc.scalar.activation(small[:, 1, cols], small[:, 3, cols], ACT.Exp, scale=-0.5).then_inc(y0_ready, 1)
                        roots[0] += 1
            transposed_hi("branch2")
            hi_lap("branch2", LAP0["branch2"] + 1)
            hi_first("out2")
            transposed_hi("out2")
            hi_lap("out2", LAP0["out2"] + 1)
            hi_first("ffn2", range(TAIL))
            norm_follows(5, lambda t: None)
            transposed_hi("ffn2", TAIL)
            swiglu("ffn2", "down2")
            for lap in range(1, LAPS["down2"]):
                hi_lap("down2", LAP0["down2"] + lap, lap % 3)

        @block.vector
        def _(dve):
            V = nc.vector
            steps = [0]
            roots = [0]

            def link(ins):
                steps[0] += 1
                ins.then_inc(dve_step, 1)
                dve.wait_ge(dve_step, steps[0])

            def refine(cols):
                y, v, a = small[:, 1, cols], small[:, 2, cols], small[:, 4, cols]
                roots[0] += 1
                dve.wait_ge(y0_ready, roots[0])
                link(V.tensor_tensor(a, y, y, ALU.mult))
                link(V.scalar_tensor_tensor(a, a, -0.5, v, ALU.mult, ALU.mult))
                return V.scalar_tensor_tensor(small[:, 5, cols], a, 1.5, y, ALU.add, ALU.mult)

            def root(n, count):
                link(V.tensor_scalar(small[:, 2, 0:n], small[:, 0, 0:n], 1.0 / count, EPS, ALU.mult, ALU.add))
                link(refine(slice(0, n)))

            def norm_tile(n, t):
                dve.wait_ge(sq_done, 4 * n + t + 1)
                link(V.tensor_scalar(small[:, 2, t:t + 1], small[:, 0, t:t + 1], 1.0 / D, EPS, ALU.mult, ALU.add))
                link(refine(slice(t, t + 1)))
                V.tensor_scalar(XN[:, t, :], X[:, t, :], small[:, 5, t:t + 1], None, ALU.mult).then_inc(xn_ready, 1)

            def norm_follows(n, before):
                for t in range(T + 1):
                    if t < T:
                        before(t)
                    if t >= 1:
                        norm_tile(n, t - 1)

            def transposed_lo(stage):
                ts = TS_OF[stage]
                for k in range(KD):
                    dve.wait_ge(ts_hi, KD * ts + k + 1)
                    V.scalar_tensor_tensor(xt_lo[:, k, :], PS[:, 4 + k % 4, :], gcol[:, ts, k:k + 1],
                                           xt_hi[:, k, :].bitcast(F32), ALU.mult, ALU.subtract).then_inc(ts_lo, 1)

            def chunk_done(stage, lap):
                dve.wait_ge(w_used, 4 * (LAP0[stage] + lap) + 4)

            def banks(s):
                return PS[:, 4 * s:4 * s + 4, :]

            def heads(ap, n):
                return ap.rearrange("p t (h d) -> p t h d", h=n)

            for t in range(T):
                norm_tile(0, t)
            dve.wait_ge(first_in, 32)
            transposed_lo("in0")

            dve.wait_ge(const_in, const_total[0])
            V.memset(gcol[:, 8, :], 1.0)
            for l in range(DEPTH):
                V.memset(gcol[:, 3 * l + 1, 4:8], 1.0)
            V.memset(gcol[:, 7, 0:4], 1.0)
            V.tensor_copy(ident_b[:, :], ident[:, :])
            V.tensor_copy(causal_b[:, :], causal_f)
            V.tensor_copy(PAIRS[:, :, :], pairs_f)
            V.tensor_copy(gcol[:, 7, 5:8], gcol[:, 7, 4:5].to_broadcast([P, 3]))
            for l in range(DEPTH):
                link(V.tensor_scalar(gcol[:, 3 * l + 1, 0:1], gcol[:, 3 * l + 1, 0:1], 1.0 - LAM_INIT[l], None, ALU.mult))
                V.tensor_copy(gcol[:, 3 * l + 1, 1:4], gcol[:, 3 * l + 1, 0:1].to_broadcast([P, 3]))
            V.tensor_scalar(qkg[:, 0:1], qkg[:, 0:1], HD ** -0.5, None, ALU.mult)
            link(V.tensor_copy(fw[:, :, :, 0:8], fw_raw))
            V.tensor_tensor(fw[:, :, :, 8:16], fw_raw, fw[:, :, :, 0:8].bitcast(F32), ALU.subtract).then_inc(fw_done, 1)
            link(V.tensor_copy(ang[:, 0, :, 0], pos_i))
            link(V.tensor_tensor(ang[:, 1], ang[:, 0, :, 0:1].to_broadcast([P, T, ROT]),
                                 freq.unsqueeze(1).to_broadcast([P, T, ROT]), ALU.mult))
            for n, quarter in ((0, 0.25), (1, 0.0)):
                link(V.tensor_scalar(ang[:, 2], ang[:, 1], 1.0 / (2 * math.pi), quarter, ALU.mult, ALU.add))
                link(V.tensor_scalar(ang[:, 3], ang[:, 2], ROUND, None, ALU.add))
                link(V.tensor_scalar(ang[:, 2], ang[:, 3], ROUND, None, ALU.subtract))
                link(V.scalar_tensor_tensor(ang[:, 4 + n], ang[:, 2], -TWO_PI[0], ang[:, 1], ALU.mult, ALU.add))
                for part in TWO_PI[1:]:
                    link(V.scalar_tensor_tensor(ang[:, 4 + n], ang[:, 2], -part, ang[:, 4 + n], ALU.mult, ALU.add))
                if quarter:
                    link(V.tensor_scalar(ang[:, 4 + n], ang[:, 4 + n], math.pi / 2, None, ALU.add))
                link(V.tensor_scalar(ang[:, 4 + n], ang[:, 4 + n], PI_F32, -PI_F32, ALU.min, ALU.max))
            q_k = lam_in.rearrange("p (a b) d -> p a b d", b=2)
            link(V.tensor_tensor(lam_t, q_k[:, :, 0, :], q_k[:, :, 1, :], ALU.mult))
            V.tensor_reduce(lam_s[:, 0:4], lam_t, AX.X, ALU.add).then_inc(lam_dots, 1)
            dve.wait_ge(lam_exps, 1)
            for l in range(DEPTH):
                link(V.tensor_tensor(lam[:, l:l + 1], lam_s[:, 4 + 2 * l:5 + 2 * l], lam_s[:, 5 + 2 * l:6 + 2 * l], ALU.subtract))
                link(V.tensor_scalar(lam[:, l:l + 1], lam[:, l:l + 1], LAM_INIT[l], -1.0, ALU.add, ALU.mult))

            def rotary(buf):
                b = heads(buf, 8)
                t1, t2 = b[:, :, :, 0:ROT], b[:, :, :, ROT:2 * ROT]
                cos, sin = (cs[:, n].unsqueeze(2).to_broadcast([P, T, 8, ROT]) for n in range(2))
                r = [rot[:, n].rearrange("p t (h d) -> p t h d", h=8) for n in range(4)]
                V.tensor_tensor(r[0], t1, cos, ALU.mult)
                V.tensor_tensor(r[1], t2, sin, ALU.mult)
                V.tensor_tensor(r[2], t2, cos, ALU.mult)
                link(V.tensor_tensor(r[3], t1, sin, ALU.mult))
                V.tensor_tensor(t1, r[0], r[1], ALU.subtract)
                link(V.tensor_tensor(t2, r[2], r[3], ALU.add))

            def attention1(l):
                stage = f"in{l}"
                dst = (QA, KA, None, QB[:, :, :, 0:HD], KB[:, :, :, 0:HD], VB[:, :, :, 0:HD])
                for c in range(6):
                    chunk_done(stage, c)
                    src = banks(c % 2)
                    if c == 2:
                        V.memset(VB[:, :, :, HD:HD + 1], 1.0)
                        V.memset(QB[:, :, :, 65:66], 8.0)
                        V.memset(KB[:, :, :, 64:65], 1.0)
                        V.tensor_copy(VA, src).then_inc(evac[0], 1)
                    elif c > 2:
                        V.tensor_copy(dst[c], heads(src, 8)).then_inc(evac[c % 2], 1)
                    else:
                        link(V.tensor_copy(dst[c], src))
                        V.memset(mark[:, c:c + 1], 1.0).then_inc(evac[c % 2], 1)
                        if l == 0 and c == 0:
                            dve.wait_ge(trig_done, 1)
                        rotary(dst[c])
                dve.wait_ge(f_turned, l + 1)
                parts = PS[:, 1, 0:T * 16].rearrange("p (t h) -> p t h", h=16)
                link(V.tensor_tensor(fy[:, 0], parts[:, :, 0:8], fbias[:, l, :].unsqueeze(1).to_broadcast([P, T, 8]), ALU.add))
                V.tensor_tensor(fy[:, 0], parts[:, :, 8:16], fy[:, 0], ALU.add).then_inc(f_biased, 1)
                dve.wait_ge(f_log, l + 1)
                V.scalar_tensor_tensor(fy[:, 2], fy[:, 0], 0.0, fy[:, 1], ALU.min, ALU.subtract).then_inc(f_gate, 1)
                for n, (src, rows, to, scale) in enumerate(items1):
                    if n == 8:
                        dve.wait_ge(c_mm, l + 1)
                        c_sum = PS[:, 0, 0:T * 8].rearrange("p (t h) -> p t h", h=8)
                        V.tensor_scalar(QB[:, :, :, 64], c_sum, 8.0, None, ALU.mult)
                        V.tensor_scalar(KB[:, :, :, 65], c_sum, -1.0, None, ALU.mult).then_inc(c_placed, 1)
                    if n % 2:
                        dve.wait_ge(tr_mm, len(items1) * l + n + 1)
                        V.tensor_scalar(to, PS[0:rows, 2 + n % 6, :], scale, None, ALU.mult).then_inc(tr_dve, 1)
                b, bo = len(units1) * l, n_out * l
                for u in range(len(units1) + OUTPUT):
                    v = u - OUTPUT
                    if v >= 0 and has_output[v]:
                        kind, (h, m), i = units1[v]
                        n = outputs(v)
                        o = PS[:, 6 + n % 2, :]
                        dve.wait_ge(o_mm, bo + n)
                        if kind == "fox":
                            r = rsum[:, v % 4:v % 4 + 1]
                            link(V.reciprocal(r, o[:, HD:HD + 1]))
                            V.tensor_scalar(MIX[:, i, CW + h * HD:CW + (h + 1) * HD], o[:, 0:HD], r, None,
                                            ALU.mult).then_inc(o_norm, 1)
                        else:
                            V.tensor_scalar(MIX[:, i, h * P:(h + 1) * P], o[:, 0:P], drec[:, (v // 2) % 8, 0:1], None,
                                            ALU.mult).then_inc(o_norm, 1)
                    if u < len(units1):
                        i = units1[u][2]
                        dve.wait_ge(s_mm, b + u + 1)
                        V.tensor_reduce(nmax[:, u % 4:u % 4 + 1], PS[:, u % 4, 0:P * (i + 1)], AX.X, ALU.max,
                                        negate=True).then_inc(max_done, 1)
                    v = u - JOIN
                    if 0 <= v < len(units1) and units1[v][0] == "diff" and has_output[v]:
                        n, pair = P * (units1[v][2] + 1), (v // 2) % 8
                        dve.wait_ge(exp_done, b + v + 1)
                        link(V.reciprocal(drec[:, pair, :], dsum[:, pair, :]))
                        link(V.scalar_tensor_tensor(mixc[:, pair:pair + 1], drec[:, pair, 1:2], dsum[:, pair, 0:1],
                                                    lam[:, l:l + 1], ALU.mult, ALU.mult))
                        V.scalar_tensor_tensor(prob[:, v % PROBS, 0:n], prob[:, v % PROBS, 0:n], mixc[:, pair:pair + 1],
                                               prob[:, (v - 1) % PROBS, 0:n], ALU.mult, ALU.add).then_inc(joined, 1)
                    if 0 <= u - DIFF_SUMS < T:
                        t = u - DIFF_SUMS
                        if t == 0:
                            dve.wait_ge(diff_sq, l + 1)
                        ins = V.tensor_reduce(small[:, 0, 4 * t:4 * t + 4], SQ[:, t, :].rearrange("p (h d) -> p h d", h=4),
                                              AX.X, ALU.add)
                        if t == T - 1:
                            ins.then_inc(ss_ready, 1)
                            dve.wait_ge(ss_ready, l + 1)
                            link(V.tensor_scalar(small[:, 2, 0:16], small[:, 0, 0:16], 1.0 / (2 * HD), EPS, ALU.mult, ALU.add))
                    if u == DIFF_ROOT + 1:
                        refine(slice(0, 16)).then_inc(diff_rstd, 1)

            def product_with_post(stage, n_post, yg):
                first = first_set(stage)

                def tile(t):
                    dve.wait_ge(half_sq, 4 * n_post + t + 1)
                    V.scalar_tensor_tensor(small[:, 2, t:t + 1], ssq[:, 1, t:t + 1], 1.0 / D, vbase[:, t:t + 1],
                                           ALU.mult, ALU.add)
                    ins = V.tensor_tensor(yg[:, t, CW:D], PS[:, 4 * (1 - first) + t, :], G[:, CW:D], ALU.mult)
                    if t < T - 1:
                        link(ins)
                    else:
                        ins.then_inc(evac[1 - first], 1)
                        dve.wait_ge(evac[1 - first], SET0[stage][1 - first] + 1)
                    link(refine(slice(t, t + 1)))
                    V.scalar_tensor_tensor(X[:, t, :], yg[:, t, :], small[:, 5, t:t + 1], X[:, t, :], ALU.mult,
                                           ALU.add).then_inc(x_ready, 1)

                chunk_done(stage, LAPS[stage] // 2 - 1)
                dve.wait_ge(gain_in, 16 * n_post + 16)
                V.tensor_tensor(yg[:, :, 0:CW], banks(first), G[:, 0:CW].unsqueeze(1).to_broadcast([P, T, CW]),
                                ALU.mult).then_inc(yg_done, 1)
                dve.wait_ge(evac[first], SET0[stage][first] + 1)
                V.tensor_scalar(vbase[:, :], ssq[:, 0, :], 1.0 / D, EPS, ALU.mult, ALU.add).then_inc(base_ready, 1)
                dve.wait_ge(base_ready, n_post + 1)
                norm_follows(n_post + 1, tile)

            def swiglu(stage):
                seen = FFN_SEEN[stage]

                def chunk_body(c, s):
                    dve.wait_ge(silu_done, seen + c + 1)
                    for j in range(2):
                        n = 2 * (seen + c) + j
                        if not (isinstance(n, int) and n == 0):
                            dve.wait_ge(h_lo, n)
                        V.tensor_tensor(h_tmp[:, :], silu_g[:, j, :], PS[:, 4 * s + 2 + j, :], ALU.mult).then_inc(h_mul, 1)
                        dve.wait_ge(h_mul, n + 1)
                        V.tensor_scalar(ht_hi[:, 2 * c + j, :], h_tmp[:, :], 1.0, None, ALU.mult).then_inc(h_hi, 1)
                        dve.wait_ge(h_hi, n + 1)
                        V.tensor_tensor(ht_lo[:, 2 * c + j, :], h_tmp[:, :], ht_hi[:, 2 * c + j, :].bitcast(F32),
                                        ALU.subtract).then_inc(h_lo, 1)

                chunk_body(0, 0)
                chunk_body(1, 1)
                with dve.Fori(1, 5) as i:
                    chunk_body(2 * i, 0)
                    chunk_body(2 * i + 1, 1)
                chunk_body(10, 0)

            for l in range(DEPTH):
                attention1(l)
                transposed_lo(f"out{l}")
                product_with_post(f"out{l}", 2 * l, YG_out)
                transposed_lo(f"ffn{l}")
                swiglu(f"ffn{l}")
                product_with_post(f"down{l}", 2 * l + 1, YG_down)
                transposed_lo(f"in{l + 1}")
            dve.wait_ge(lb_in, 16)
            link(V.tensor_tensor(lb_tmp[:, 2, :], lb_tmp[:, 0, :], lb_tmp[:, 1, :], ALU.max))
            V.tensor_tensor(lb_tmp[:, 0:2, :], lb_tmp[:, 0:2, :], lb_tmp[:, 2:3, :].to_broadcast([P, 2, CW]),
                            ALU.subtract).then_inc(lb_max, 1)
            dve.wait_ge(lb_exp, 1)
            link(V.tensor_tensor(lb_tmp[:, 2, :], lb_tmp[:, 0, :], lb_tmp[:, 1, :], ALU.add))
            link(V.reciprocal(lb_tmp[:, 3, :], lb_tmp[:, 2, :]))
            link(V.tensor_tensor(G2[:, 0, :], lb_tmp[:, 0, :], lb_tmp[:, 3, :], ALU.mult))
            link(V.tensor_scalar(G2[:, 1, :], G2[:, 0, :], -1.0, 1.0, ALU.mult, ALU.add))

            for c in range(7):
                if c in (0, 1):
                    buf = (QS, KS)[c]
                    chunk_done("in2", c)
                    link(V.tensor_copy(buf, banks(c)))
                    V.memset(mark[:, c:c + 1], 1.0).then_inc(evac[c], 1)
                    V.memset(mark[:, 2:3], 1.0).then_inc(qk_copied, 1)
                    dve.wait_ge(qk_sq, c + 1)
                    V.tensor_reduce(small[:, 0, 0:32].rearrange("p (t h) -> p t h", h=8), heads(SQ2, 8), AX.X,
                                    ALU.add).then_inc(ss_ready, 1)
                    dve.wait_ge(ss_ready, DEPTH + c + 1)
                    root(32, HD)
                    flat = buf.rearrange("p t (h d) -> p (t h) d", d=HD)
                    V.tensor_tensor(flat, flat, small[:, 5, 0:32].unsqueeze(2).to_broadcast([P, 32, HD]), ALU.mult)
                elif c in (2, 5):
                    chunk_done("in2", c)
                    V.tensor_copy((VS if c == 2 else VAL), banks(c % 2)).then_inc(evac[c % 2], 1)
                elif c in (3, 6):
                    buf = QH if c == 3 else GG
                    dve.wait_ge(sig_done, {3: 1, 6: 3}[c])
                    V.tensor_tensor(buf, buf, banks(c % 2), ALU.mult).then_inc(evac[c % 2], 1)
                else:
                    dve.wait_ge(sig_done, 2)
                    V.memset(mark[:, 3:4], 1.0).then_inc(evac[0], 1)
                    link(V.tensor_tensor(LOGF, KEY, G2[:, 1:2, :].to_broadcast([P, T, CW]), ALU.mult))
                    link(V.tensor_tensor(LOGF, LOGF, G2[:, 0:1, :].to_broadcast([P, T, CW]), ALU.add))
                    link(V.tensor_scalar(KEY, LOGF, -1.0, 1.0, ALU.mult, ALU.add))
                    V.tensor_scalar(LOGF, LOGF, 2.0 ** -62, None, ALU.max).then_inc(f_sum, 1)
            V.memset(mark[:, 2:3], 1.0).then_inc(qk2_done, 1)
            for n, (src, rows, to, scale) in enumerate(items2):
                if n % 2:
                    dve.wait_ge(tr_mm, 2 * len(items1) + n + 1)
                    V.tensor_scalar(to, PS[:, n % 8, :], scale, None, ALU.mult).then_inc(tr_dve, 1)

            for u in range(len(units2) + 5):
                if u < len(units2):
                    h, j = units2[u]
                    n = SEQ - P * j
                    z = PS[:, u % 3, 0:n]
                    lt = sb_l[u % 6][:, 0:n]
                    sp = sb_sp[:, h % 2, sp_at[j]:sp_at[j] + n]
                    dve.wait_ge(l_done, u + 1)
                    link(V.scalar_tensor_tensor(sp, z, 0.0, lt, ALU.max, ALU.add))
                    V.tensor_tensor(sp[:, 0:P], sp[:, 0:P], SUMS[:, BEFORE, :], ALU.mult)
                    V.scalar_tensor_tensor(lt, z, 0.0, lt, ALU.min, ALU.subtract).then_inc(sp_done, 1)
                v = u - 2
                if 0 <= v < len(units2):
                    h, j = units2[v]
                    n = SEQ - P * j
                    lt = sb_l[v % 6][:, 0:n]
                    dve.wait_ge(rest_mm, v + 1)
                    V.tensor_tensor(lt, lt, PS[:, 3 + v % 3, 0:n], ALU.subtract).then_inc(arg_done, 1)
                v = u - 5
                if v >= 0 and units2[v][1] == 0:
                    h = units2[v][0]
                    dve.wait_ge(av_mm, v + 1)
                    V.tensor_copy(MIX[:, :, h * HD:(h + 1) * HD],
                                  PS[:, 6 + h % 2, 0:T * HD].rearrange("p (t d) -> p t d", d=HD)).then_inc(av_ev, 1)

            for u in range(len(hg_units) + 3):
                if u < len(hg_units):
                    i, h = hg_units[u]
                    dve.wait_ge(e_exp, u + 1)
                    if u >= 2:
                        dve.wait_ge(oh_mm, u - 1)
                    if i < T - 1:
                        V.tensor_copy(dtot[:, u % 4:u % 4 + 1], hg_e[u % 2][:, UPTO, P - 1:P])
                    V.tensor_tensor(hg_q[u % 2], hg_e[u % 2][:, 0:LEVELS + 1, :],
                                    QHT[:, h, i * P:(i + 1) * P].unsqueeze(1).to_broadcast([P, LEVELS + 1, P]),
                                    ALU.mult).then_inc(qe_done, 1)
                v = u - 1
                if 0 <= v < len(hg_units):
                    dve.wait_ge(a_mm, v + 1)
                    if v >= 1:
                        dve.wait_ge(a_sum, v)
                    V.tensor_tensor(hg_a, psum_a, PAIRS[:, :, :], ALU.mult).then_inc(a_read, 1)
                    dve.wait_ge(a_read, v + 1)
                    V.tensor_reduce(hg_at[:, v % 2, :], hg_a.rearrange("p l t -> p t l"), AX.X, ALU.add).then_inc(a_sum, 1)
                v = u - 2
                if 0 <= v < len(hg_units) and hg_units[v][0] < T - 1:
                    i, h = hg_units[v]
                    dve.wait_ge(kv_mm, v + 1)
                    dve.wait_ge(oh_mm, v + 1)
                    st = hg_state[:, h, :]
                    if i == 0:
                        V.tensor_copy(st, PS[:, 7, 0:P]).then_inc(state_done, 1)
                    else:
                        V.scalar_tensor_tensor(st, st, dtot[:, v % 4:v % 4 + 1], PS[:, 7, 0:P], ALU.mult,
                                               ALU.add).then_inc(state_done, 1)
                v = u - 3
                if v >= 0 and hg_units[v][1] == 3:
                    i = hg_units[v][0]
                    cols = slice(4 * i, 4 * i + 4)
                    dve.wait_ge(oh_ev, v + 1)
                    link(V.tensor_scalar(small[:, 2, cols], small[:, 0, cols], 1.0 / P, EPS, ALU.mult, ALU.add))
                    link(refine(cols))
                    for h in range(4):
                        part = MIX[:, i, CW + h * P:CW + (h + 1) * P]
                        ins = V.scalar_tensor_tensor(part, part, small[:, 5, 4 * i + h:4 * i + h + 1],
                                                     GG[:, i, h * P:(h + 1) * P], ALU.mult, ALU.mult)
                    ins.then_inc(xn_ready, 1)
            transposed_lo("branch2")

            for q in range(4):
                cols = slice((q // 2) * CW, (q // 2 + 1) * CW)
                gate = (GATE_SB, GATE_HG)[q % 2][:, :, cols]
                dve.wait_ge(w_used, 4 * LAP0["branch2"] + 2 * q + 2)
                V.tensor_tensor(gate, gate, banks(q % 2), ALU.mult).then_inc(evac[q % 2], 1)
                if q % 2:
                    dve.wait_ge(evac[1], SET0["branch2"][1] + q // 2 + 1)
                    for t in range(T):
                        ins = V.tensor_tensor(GATE_SB[:, t, cols], GATE_SB[:, t, cols], GATE_HG[:, t, cols], ALU.add)
                        if q == 3:
                            ins.then_inc(xn_ready, 1)
            transposed_lo("out2")
            chunk_done("out2", 0)
            V.tensor_tensor(X[:, :, 0:CW], X[:, :, 0:CW], banks(0), ALU.add).then_inc(evac[0], 1)

            def out2_tile(t):
                wait_tile(dve, "out2", t)
                V.tensor_tensor(X[:, t, CW:D], X[:, t, CW:D], PS[:, 4 + t, :], ALU.add).then_inc(x_ready, 1)

            norm_follows(5, out2_tile)
            transposed_lo("ffn2")
            swiglu("ffn2")
            chunk_done("down2", 2)
            V.tensor_tensor(X[:, :, 0:CW], X[:, :, 0:CW], banks(1), ALU.add).then_inc(final_ready, 1)
            for t in range(T):
                wait_tile(dve, "down2", t)
                V.tensor_tensor(X[:, t, CW:D], X[:, t, CW:D], PS[:, t, :], ALU.add).then_inc(final_ready, 1)

        @block.tensor
        def _(pe):
            mm = nc.tensor.matmul

            def three(out_, a_hi, a_lo, b_hi, b_lo, start, stop):
                mm(out_, a_hi, b_hi, start=start, stop=False)
                mm(out_, a_hi, b_lo, start=False, stop=False)
                return mm(out_, a_lo, b_hi, start=False, stop=stop)

            def turn(stage, k, t):
                ins = nc.tensor.transpose(PS[:, 4 + k % 4, t * P:(t + 1) * P],
                                          SOURCE[stage][:, t, k * P:(k + 1) * P], ident[:, :])
                if t == T - 1:
                    ins.then_inc(ts_mm, 1)

            def transposed_start(stage):
                if SET0[stage][1]:
                    pe.wait_ge(evac[1], SET0[stage][1])
                for t in range(T):
                    pe.wait_ge(xn_ready, T * TS_OF[stage] + t + 1)
                    for k in range(4):
                        turn(stage, k, t)

            def transposed_next(stage, k):
                if k < 4:
                    pe.wait_ge(ts_lo, KD * TS_OF[stage] + k + 1)
                    for t in range(T):
                        turn(stage, k + 4, t)

            SOURCE = {"in0": XN, "ffn0": XN, "in1": XN, "ffn1": XN, "in2": XN, "ffn2": XN,
                      "out0": MIX, "out1": MIX, "branch2": MIX, "out2": GATE_SB}

            def set_free(stage, c, s):
                n = SET0[stage][s] + c // 2 if isinstance(c, int) else SET0[stage][s] + c
                if not (isinstance(n, int) and n == 0):
                    pe.wait_ge(evac[s], n)

            def use_slot(r, sub, out_banks, a_hi, a_lo, start, stop):
                for t in range(T):
                    tok = slice(t * P, (t + 1) * P)
                    last = three(out_banks[:, t, :], a_hi[:, tok], a_lo[:, tok], w_hi[:, r, sub, :], w_lo[:, r, sub, :],
                                 start, stop)
                return last

            def token_chunk(stage, lap, s, laps, first, tiled=False):
                a_hi, a_lo = (ht_hi, ht_lo) if is_down(stage) else (xt_hi, xt_lo)
                kn = KF if is_down(stage) else KD
                tail = (laps - 1, TAIL) if tiled else (laps, 0)
                k = 0
                for lap3 in range(laps):
                    for r, subs in enumerate(lap_subs(stage, lap3)):
                        if (lap3, r) >= tail:
                            break
                        pe.wait_ge(lo_ready, 4 * (lap + lap3) + r + 1)
                        for sub in range(subs):
                            if first and not is_down(stage):
                                pe.wait_ge(ts_lo, KD * TS_OF[stage] + k + 1)
                            if first and is_down(stage) and k >= KF - 4:
                                pe.wait_ge(h_lo, KF * (TILED.index(stage) // 2) + k + 1)
                            last = use_slot(r, sub, PS[:, 4 * s:4 * s + 4, :], a_hi[:, k, :], a_lo[:, k, :],
                                            k == 0, k == kn - 1)
                            if sub == subs - 1:
                                last.then_inc(w_used, 1)
                            if first and not is_down(stage):
                                transposed_next(stage, k)
                            k += 1
                if not tiled:
                    return
                k0 = k
                for t in range(T):
                    tok = slice(t * P, (t + 1) * P)
                    k = k0
                    for r in range(tail[1], R):
                        if t == 0:
                            pe.wait_ge(lo_ready, 4 * (lap + laps - 1) + r + 1)
                        for sub in range(lap_subs(stage, laps - 1)[r]):
                            last = three(PS[:, 4 * s + t, :], a_hi[:, k, tok], a_lo[:, k, tok], w_hi[:, r, sub, :],
                                         w_lo[:, r, sub, :], False, k == kn - 1)
                            k += 1
                        if t == T - 1:
                            last.then_inc(w_used, 1)
                    if t < T - 1:
                        last.then_inc(tile_done, 1)

            def project(stage):
                n = LAPS[stage]
                for c in range(2):
                    set_free(stage, c, c)
                    token_chunk(stage, LAP0[stage] + c, c, 1, c == 0)
                with pe.Fori(1, n // 2) as i:
                    for s in range(2):
                        pe.wait_ge(evac[s], SET0[stage][s] + i)
                        token_chunk(stage, LAP0[stage] + 2 * i + s, s, 1, False)
                if n % 2:
                    set_free(stage, n - 1, 0)
                    token_chunk(stage, LAP0[stage] + n - 1, 0, 1, False)

            def two_chunks(stage):
                laps = LAPS[stage] // 2
                for c in range(2):
                    s = c ^ first_set(stage)
                    set_free(stage, c, s)
                    token_chunk(stage, LAP0[stage] + c * laps, s, laps, c == 0, c == 1)

            def swiglu(stage):
                seen = FFN_SEEN[stage]

                def chunk(c, s, first):
                    if not (isinstance(c, int) and c < 2):
                        pe.wait_ge(h_mul, 2 * (seen + c) - 2)
                    elif c == 0:
                        pe.wait_ge(evac[0], SET0[stage][0])
                    for r in range(R):
                        pe.wait_ge(lo_ready, 4 * (LAP0[stage] + c) + r + 1)
                        for sub in range(2):
                            k = 2 * r + sub
                            if first:
                                pe.wait_ge(ts_lo, KD * TS_OF[stage] + k + 1)
                            for j in range(4):
                                cols = slice(j * P, (j + 1) * P)
                                last = three(PS[:, 4 * s + j, :], w_hi[:, r, sub, cols], w_lo[:, r, sub, cols],
                                             xt_hi[:, k, :], xt_lo[:, k, :], k == 0, k == KD - 1)
                            if sub == 1:
                                last.then_inc(w_used, 1)
                            if first:
                                transposed_next(stage, k)

                chunk(0, 0, True)
                chunk(1, 1, False)
                with pe.Fori(1, 5) as i:
                    chunk(2 * i, 0, False)
                    chunk(2 * i + 1, 1, False)
                chunk(10, 0, False)
                pe.wait_ge(h_mul, 2 * (seen + 10))

            def transpose_item(n, base, items, bank, reuse):
                src, rows, _, _ = items[n]
                m = n - reuse
                if m >= 0:
                    done = base // 2 + m // 2 + 1
                    pe.wait_ge(tr_dve if m % 2 else tr_act, done)
                for t in range(T):
                    last = nc.tensor.transpose(PS[0:rows, bank, t * P:(t + 1) * P], src[:, t, :], ident[:, :])
                last.then_inc(tr_mm, 1)

            def attention1(l):
                stage = f"in{l}"
                pe.wait_ge(evac[0], SET0[stage][0] + 3)
                pe.wait_ge(fw_done, 1)
                for k in range(KD):
                    mm(PS[0:16, 0, :], fw[:, l, k, :], xt_hi[:, k, :], start=k == 0, stop=False)
                    last = mm(PS[0:16, 0, :], fw[:, l, k, :], xt_lo[:, k, :], start=False, stop=k == KD - 1)
                last.then_inc(f_mm, 1)
                pe.wait_ge(evac[1], SET0[stage][1] + 3)
                base = len(items1) * l
                for n in range(8):
                    if n == 2:
                        pe.wait_ge(f_copied, l + 1)
                        for t in range(T):
                            last = nc.tensor.transpose(PS[:, 1, 16 * t:16 * t + 16], f_rows[:, t * P:(t + 1) * P],
                                                       ident[0:16, 0:16])
                        last.then_inc(f_turned, 1)
                    transpose_item(n, base, items1, 2 + n % 6, 6)
                pe.wait_ge(f_gate, l + 1)
                mm(PS[:, 0, 0:8 * T], SUMS[:, UPTO, :], fy[:, 2, :, :], start=True, stop=False)
                for back in range(1, T):
                    last = mm(PS[:, 0, 8 * back:8 * T], SUMS[:, ONES, :], fy[:, 2, 0:T - back, :],
                              start=False, stop=back == T - 1)
                last.then_inc(c_mm, 1)
                pe.wait_ge(c_placed, l + 1)
                for n in range(8, len(items1)):
                    transpose_item(n, base, items1, 2 + n % 6, 6)
                pe.wait_ge(tr_act, (base + len(items1)) // 2)
                pe.wait_ge(tr_dve, (base + len(items1)) // 2)
                b, bo, bj = len(units1) * l, n_out * l, n_join * l
                for u in range(len(units1) + PRODUCT):
                    v = u - TURN
                    if 0 <= v < len(units1) and has_output[v]:
                        i = units1[v][2]
                        n = outputs(v)
                        if units1[v][0] == "diff":
                            pe.wait_ge(joined, bj + joins(v))
                        else:
                            pe.wait_ge(exp_done, b + v + 1)
                        if bo + n > 2:
                            pe.wait_ge(pt_ev, bo + n - 2)
                        for j in range(i + 1):
                            last = nc.tensor.transpose(PS[:, 4 + n % 2, j * P:(j + 1) * P],
                                                       prob[:, v % PROBS, j * P:(j + 1) * P], ident[:, :])
                        last.then_inc(pt_mm, 1)
                    if u < len(units1):
                        kind, (h, m), i = units1[u]
                        tok, upto = slice(i * P, (i + 1) * P), P * (i + 1)
                        if kind == "diff":
                            q, kk = QAT[64 * m:64 * m + 64, h, tok], KAT[64 * m:64 * m + 64, h, 0:upto]
                        else:
                            q, kk = QBT[0:66, h, tok], KBT[0:66, h, 0:upto]
                        if b + u >= 4:
                            pe.wait_ge(exp_done, b + u - 3)
                        mm(PS[:, u % 4, 0:upto], q, kk, start=True, stop=False)
                        mm(PS[:, u % 4, upto - P:upto], ident_b[:, :], causal_b[:, :], start=False, stop=True).then_inc(s_mm, 1)
                    v = u - PRODUCT
                    if v >= 0 and has_output[v]:
                        kind, (h, m), i = units1[v]
                        n = outputs(v)
                        pe.wait_ge(pt_ev, bo + n)
                        if bo + n > 2:
                            pe.wait_ge(o_norm, bo + n - 2)
                        for j in range(i + 1):
                            vals, width = (VA[:, j, h * P:(h + 1) * P], P) if kind == "diff" else (VB[:, j, h, :], HD + 1)
                            last = mm(PS[:, 6 + n % 2, 0:width], probT[:, n % 2, j * P:(j + 1) * P], vals,
                                      start=j == 0, stop=j == i)
                        last.then_inc(o_mm, 1)

            pe.wait_ge(first_in, 32)
            transposed_start("in0")
            for l in range(DEPTH):
                project(f"in{l}")
                attention1(l)
                pe.wait_ge(o_norm, n_out * (l + 1))
                transposed_start(f"out{l}")
                two_chunks(f"out{l}")
                transposed_start(f"ffn{l}")
                swiglu(f"ffn{l}")
                two_chunks(f"down{l}")
                transposed_start(f"in{l + 1}")

            project("in2")
            pe.wait_ge(evac[0], SET0["branch2"][0])
            pe.wait_ge(evac[1], SET0["branch2"][1])
            pe.wait_ge(qk2_done, 1)
            for n in range(len(items2)):
                transpose_item(n, 2 * len(items1), items2, n % 8, 8)
            pe.wait_ge(tr_act, len(items1) + len(items2) // 2)
            pe.wait_ge(tr_dve, len(items1) + len(items2) // 2)
            for u in range(len(units2) + 4):
                if u < len(units2):
                    h, j = units2[u]
                    n = SEQ - P * j
                    rows = slice(64 * (h % 2), 64 * (h % 2) + 64)
                    if u >= 3:
                        pe.wait_ge(sp_done, u - 2)
                    mm(PS[:, u % 3, 0:n], KST[rows, h // 2, j * P:(j + 1) * P], QST[rows, h // 2, j * P:SEQ],
                       start=True, stop=True).then_inc(z_mm, 1)
                v = u - 2
                if 0 <= v < len(units2):
                    h, j = units2[v]
                    n = SEQ - P * j
                    pe.wait_ge(sp_done, v + 1)
                    if v >= 3:
                        pe.wait_ge(arg_done, v - 2)
                    for jj in range(j, T):
                        m = SEQ - P * jj
                        last = mm(PS[:, 3 + v % 3, n - m:n], SUMS[:, AFTER if jj == j else ONES, :],
                                  sb_sp[:, h % 2, sp_at[jj]:sp_at[jj] + m], start=jj == j, stop=jj == T - 1)
                    last.then_inc(rest_mm, 1)
                v = u - 4
                if v >= 0:
                    h, j = units2[v]
                    pe.wait_ge(w_mask, v + 1)
                    if j == T - 1 and h >= 2:
                        pe.wait_ge(av_ev, h - 1)
                    for i in range(j, T):
                        last = mm(PS[:, 6 + h % 2, i * HD:(i + 1) * HD], sb_l[v % 6][:, (i - j) * P:(i - j + 1) * P],
                                  VS[:, j, h * HD:(h + 1) * HD], start=j == T - 1, stop=j == 0, skip_group_check=True)
                    last.then_inc(av_mm, 1)
            pe.wait_ge(av_ev, 8)
            pe.wait_ge(log_done, 1)
            for u in range(len(hg_units) + 2):
                if u < len(hg_units):
                    i, h = hg_units[u]
                    if u >= 1:
                        pe.wait_ge(e_exp, u)
                    lf = LOGF[:, i, h * P:(h + 1) * P]
                    for bank in range(3):
                        w = min(4, NE - 4 * bank)
                        last = mm(PS[:, bank, 0:w * P], lf, SUMS[:, 4 * bank:4 * bank + w, :], start=True, stop=True)
                    last.then_inc(e_mm, 1)
                v = u - 1
                if 0 <= v < len(hg_units):
                    i, h = hg_units[v]
                    tok = slice(i * P, (i + 1) * P)
                    pe.wait_ge(qe_done, v + 1)
                    pe.wait_ge(ke_done, v + 1)
                    if v >= 1:
                        pe.wait_ge(a_read, v)
                    for l in range(LEVELS + 1):
                        kk = KHT[:, h, tok] if l == 0 else hg_k[v % 2][:, l - 1, :]
                        q = QHT[:, h, tok] if l == 0 else hg_q[v % 2][:, l, :]
                        last = mm(psum_a[:, l, :], kk, q, start=True, stop=True)
                    last.then_inc(a_mm, 1)
                    if i < T - 1:
                        if v >= 1:
                            pe.wait_ge(ket_ev, v)
                        nc.tensor.transpose(PS[:, 5, 0:P], hg_k[v % 2][:, LEVELS, :], ident[:, :]).then_inc(ket_mm, 1)
                v = u - 2
                if v >= 0:
                    i, h = hg_units[v]
                    val = VAL[:, i, h * P:(h + 1) * P]
                    if i < T - 1:
                        pe.wait_ge(ket_ev, v + 1)
                        if v >= 1:
                            pe.wait_ge(state_done, v)
                        mm(PS[:, 7, 0:P], hg_ket[:, v % 2, :], val, start=True, stop=True).then_inc(kv_mm, 1)
                    pe.wait_ge(a_sum, v + 1)
                    if v >= 1:
                        pe.wait_ge(oh_ev, v)
                    last = mm(PS[:, 6, 0:P], hg_at[:, v % 2, :], val, start=True, stop=i == 0)
                    if i > 0:
                        pe.wait_ge(state_done, 4 * (i - 1) + h + 1)
                        last = mm(PS[:, 6, 0:P], hg_q[v % 2][:, UPTO, :], hg_state[:, h, :], start=False, stop=True)
                    last.then_inc(oh_mm, 1)
            pe.wait_ge(oh_ev, len(hg_units))
            pe.wait_ge(state_done, states_before(len(hg_units)))
            transposed_start("branch2")
            for q in range(4):
                half = q % 2
                set_free("branch2", q, half)
                for r in (2 * half, 2 * half + 1):
                    pe.wait_ge(lo_ready, 4 * (LAP0["branch2"] + q // 2) + r + 1)
                    for sub in range(2):
                        k = 2 * r + sub
                        if q < 2:
                            pe.wait_ge(ts_lo, KD * TS_OF["branch2"] + (k if q == 0 else KD - 1) + 1)
                        last = use_slot(r, sub, PS[:, 4 * half:4 * half + 4, :], xt_hi[:, k, :], xt_lo[:, k, :],
                                        k % 4 == 0, k % 4 == 3)
                        if sub == 1:
                            last.then_inc(w_used, 1)
                        if q == 0:
                            transposed_next("branch2", k)
            transposed_start("out2")
            two_chunks("out2")
            pe.wait_ge(x_ready, 4 * 5)
            transposed_start("ffn2")
            swiglu("ffn2")
            two_chunks("down2")


_INS = ["x", "positions", "attn_pre_g", "w_in", "forget_bias", "lam_q1", "lam_k1", "lam_q2", "lam_k2", "diff_sub_g",
        "w_out", "attn_post_g", "ffn_pre_g", "w_gate", "w_up", "w_down", "ffn_post_g", "norm1_g_2", "w_in_2",
        "q_norm_g_2", "k_norm_g_2", "lb_table_2", "hg_norm_g_2", "w_branch_2", "w_out_2", "norm2_g_2",
        "w_ffn_gate_2", "w_ffn_up_2", "w_ffn_down_2"]


def kernel(**inputs):
    import concourse.bacc as bacc
    from concourse.bass_utils import run_bass_kernel_spmd

    nc = bacc.Bacc("TRN2", target_bir_lowering=False, num_devices=1)
    arrays, args = {}, []
    for name in _INS:
        arrays[f"in_{name}"] = np.ascontiguousarray(inputs[name])
    for name, table in shape_constants().items():
        arrays[f"in_{name}"] = np.ascontiguousarray(table)
    for name, a in arrays.items():
        args.append(nc.dram_tensor(name, a.shape, mybir.dt.from_np(a.dtype), kind="ExternalInput").ap())
    args.append(nc.dram_tensor("out_0", (1, SEQ, D), F32, kind="ExternalOutput").ap())
    build(nc, *args)
    r = run_bass_kernel_spmd(nc, [arrays], core_ids=[0])
    return r.results[0]["out_0"]
```
